# Optimizing a Trainium2 kernel written in Bass

```python
import math
import jax, jax.numpy as jnp
from jax import lax
import numpy as np

D_MODEL = 1024
BATCH = 1
SEQ = 512
DEPTH = 1

D_MIX = D_MODEL
D_ATTN = D_MIX // 2
D_POOL = D_MIX - D_ATTN
HEAD_DIM = 64
ATTN_HEADS = D_ATTN // HEAD_DIM
DILATED_PATTERNS = ((128, 1), (512, 4), (2048, 16))
WBLK = 128
POOL_WINDOWS = (2, 4, 8, 16)
N_POOL_GROUPS = len(POOL_WINDOWS)
POOL_GROUP_DIM = D_POOL // N_POOL_GROUPS
PEER_HEADS = 8
N_KEYS = 128
N_EXPERTS = N_KEYS * N_KEYS
PEER_TOPK = 16
PEER_QDIM = 256
PEER_HALF = PEER_QDIM // 2
TOKEN_CHUNK = 128
EPS = 1e-6
NEG = -1e30

kernel_name = "hymba_dilated_pool_peer_block"

def rmsnorm(x, g):
    xf = x.astype(jnp.float32)
    y = xf * lax.rsqrt(jnp.mean(xf * xf, axis=-1, keepdims=True) + EPS)
    return (y * g.astype(jnp.float32)).astype(x.dtype)

def dilated_branch(q, k, v, window, dilation):
    b, s, h, dh = q.shape
    n_steps = window // dilation
    L = s // dilation
    nb = -(-L // WBLK)
    Lp = nb * WBLK

    def to_sub(t):
        t = t.reshape(b, L, dilation, h, dh).transpose(0, 2, 3, 1, 4)
        t = jnp.pad(t, ((0, 0), (0, 0), (0, 0), (0, Lp - L), (0, 0)))
        return t.reshape(b, dilation, h, nb, WBLK, dh)

    def with_prev(t):
        prev = jnp.pad(t, ((0, 0), (0, 0), (0, 0), (1, 0), (0, 0), (0, 0)))[:, :, :, :nb]
        return jnp.concatenate([prev, t], axis=4)

    qb = to_sub(q)
    kx = with_prev(to_sub(k))
    vx = with_prev(to_sub(v))
    scores = jnp.einsum('brhnqd,brhnkd->brhnqk', qb, kx).astype(jnp.float32) * (dh ** -0.5)
    qi = jnp.arange(WBLK)[:, None]
    kj = jnp.arange(2 * WBLK)[None, :]
    dist = qi + WBLK - kj
    kpos = jnp.arange(nb)[:, None, None] * WBLK - WBLK + kj[None]
    mask = (dist >= 0)[None] & (dist <= n_steps)[None] & (kpos >= 0)
    scores = jnp.where(mask[None, None, None], scores, NEG)
    m = jnp.max(scores, axis=-1, keepdims=True)
    p = jnp.exp(scores - m)
    den = jnp.sum(p, axis=-1, keepdims=True)
    o = jnp.einsum('brhnqk,brhnkd->brhnqd', p, vx.astype(jnp.float32)) / den
    lse = (m + jnp.log(den))[..., 0]
    o = o.reshape(b, dilation, h, Lp, dh)[:, :, :, :L].transpose(0, 3, 1, 2, 4).reshape(b, s, h, dh)
    lse = lse.reshape(b, dilation, h, Lp)[..., :L].transpose(0, 3, 1, 2).reshape(b, s, h)
    return o, lse

def dilated_attention(q, k, v):
    outs, lses = [], []
    for window, dilation in DILATED_PATTERNS:
        o, lse = dilated_branch(q, k, v, window, dilation)
        outs.append(o)
        lses.append(lse)
    w = jax.nn.softmax(jnp.stack(lses, axis=0), axis=0)
    o = jnp.sum(w[..., None] * jnp.stack(outs, axis=0), axis=0)
    return o.astype(q.dtype)

def pool_mixer(z, w_pool, pool_scale):
    b, s, c = z.shape
    zg = z.astype(jnp.float32).reshape(b, s, N_POOL_GROUPS, POOL_GROUP_DIM)
    cs = jnp.cumsum(zg, axis=1)
    t = jnp.arange(1, s + 1, dtype=jnp.float32)
    outs = []
    for g, win in enumerate(POOL_WINDOWS):
        csg = cs[:, :, g]
        lag = jnp.pad(csg, ((0, 0), (win, 0), (0, 0)))[:, :s]
        mean = (csg - lag) / jnp.minimum(t, float(win))[None, :, None]
        outs.append(mean - zg[:, :, g])
    pooled = jnp.stack(outs, axis=2)
    mixed = jnp.einsum('bsgc,gcd->bsgd', pooled, w_pool.astype(jnp.float32)).reshape(b, s, c)
    return (mixed * pool_scale.astype(jnp.float32)).astype(z.dtype)

def peer(h, w_query, sub_keys, expert_u, expert_v):
    b, s, d = h.shape
    q = jnp.einsum('bsd,de->bse', h, w_query).reshape(b, s, PEER_HEADS, 2, PEER_HALF)
    sc = jnp.einsum('bshpc,hpkc->bshpk', q, sub_keys).astype(jnp.float32)
    top_s, top_i = lax.top_k(sc, PEER_TOPK)
    cand_s = top_s[..., 0, :, None] + top_s[..., 1, None, :]
    cand_i = top_i[..., 0, :, None] * N_KEYS + top_i[..., 1, None, :]
    kk = PEER_TOPK * PEER_TOPK
    best_s, best_pos = lax.top_k(cand_s.reshape(b, s, PEER_HEADS, kk), PEER_TOPK)
    expert_idx = jnp.take_along_axis(cand_i.reshape(b, s, PEER_HEADS, kk), best_pos, axis=-1)
    gates = jax.nn.softmax(best_s, axis=-1)
    n_chunks = (b * s) // TOKEN_CHUNK
    xc = h.reshape(n_chunks, TOKEN_CHUNK, d)
    ic = expert_idx.reshape(n_chunks, TOKEN_CHUNK, PEER_HEADS, PEER_TOPK)
    gc = gates.reshape(n_chunks, TOKEN_CHUNK, PEER_HEADS, PEER_TOPK)

    def chunk_fn(args):
        xt, it, gt = args
        u = expert_u[it]
        a = jnp.einsum('chkd,cd->chk', u, xt).astype(jnp.float32)
        act = jax.nn.gelu(a, approximate=False) * gt
        vsel = expert_v[it]
        return jnp.einsum('chk,chkd->cd', act, vsel.astype(jnp.float32))

    y = lax.map(chunk_fn, (xc, ic, gc))
    return y.reshape(b, s, d).astype(h.dtype)

def setup_inputs(seed: int = 0) -> dict:
    key = jax.random.key(seed)
    ks = jax.random.split(key, 13)
    f32 = jnp.float32
    x = jax.random.normal(ks[0], (BATCH, SEQ, D_MODEL), f32)
    norm_mix = 1.0 + 0.1 * jax.random.normal(ks[1], (DEPTH, D_MODEL), f32)
    w_in = jax.random.normal(ks[2], (DEPTH, D_MODEL, 3 * D_ATTN + D_POOL), f32) * D_MODEL ** -0.5
    w_pool = jax.random.normal(ks[3], (DEPTH, N_POOL_GROUPS, POOL_GROUP_DIM, POOL_GROUP_DIM), f32) * POOL_GROUP_DIM ** -0.5
    pool_scale = 1.0 + 0.1 * jax.random.normal(ks[4], (DEPTH, D_POOL), f32)
    w_out = jax.random.normal(ks[5], (DEPTH, D_MIX, D_MODEL), f32) * D_MIX ** -0.5
    norm_ffn = 1.0 + 0.1 * jax.random.normal(ks[6], (DEPTH, D_MODEL), f32)
    w_query = jax.random.normal(ks[7], (DEPTH, D_MODEL, PEER_HEADS * PEER_QDIM), f32) * D_MODEL ** -0.5
    sub_keys = jax.random.normal(ks[8], (DEPTH, PEER_HEADS, 2, N_KEYS, PEER_HALF), f32) * PEER_HALF ** -0.5
    expert_u = jax.random.normal(ks[9], (DEPTH, N_EXPERTS, D_MODEL), f32) * D_MODEL ** -0.5
    expert_v = jax.random.normal(ks[10], (DEPTH, N_EXPERTS, D_MODEL), f32) * PEER_TOPK ** -0.5
    norm_final = 1.0 + 0.1 * jax.random.normal(ks[11], (D_MODEL,), f32)
    return {"x": x, "norm_mix": norm_mix, "w_in": w_in, "w_pool": w_pool, "pool_scale": pool_scale,
            "w_out": w_out, "norm_ffn": norm_ffn, "w_query": w_query, "sub_keys": sub_keys,
            "expert_u": expert_u, "expert_v": expert_v, "norm_final": norm_final}

def reference(x, norm_mix, w_in, w_pool, pool_scale, w_out, norm_ffn, w_query, sub_keys,
              expert_u, expert_v, norm_final):
    b, s, _ = x.shape
    for layer in range(DEPTH):
        h = rmsnorm(x, norm_mix[layer])
        z = jnp.einsum('bsd,de->bse', h, w_in[layer])
        q = z[..., :D_ATTN].reshape(b, s, ATTN_HEADS, HEAD_DIM)
        k = z[..., D_ATTN:2 * D_ATTN].reshape(b, s, ATTN_HEADS, HEAD_DIM)
        v = z[..., 2 * D_ATTN:3 * D_ATTN].reshape(b, s, ATTN_HEADS, HEAD_DIM)
        zp = z[..., 3 * D_ATTN:]
        att = dilated_attention(q, k, v).reshape(b, s, D_ATTN)
        pooled = pool_mixer(zp, w_pool[layer], pool_scale[layer])
        mix = jnp.concatenate([att, pooled], axis=-1)
        x = x + jnp.einsum('bse,ed->bsd', mix, w_out[layer])
        hf = rmsnorm(x, norm_ffn[layer])
        x = x + peer(hf, w_query[layer], sub_keys[layer], expert_u[layer], expert_v[layer])
    return rmsnorm(x, norm_final)


_drawn_inputs = setup_inputs


def setup_inputs(seed=0):
    import zlib

    import numpy as np

    out = dict(_drawn_inputs(seed))
    spreads = {}
    factors = {}
    for name, (base, spread) in spreads.items():
        noise = np.random.default_rng([zlib.crc32(name.encode()), seed]).standard_normal(out[name].shape)
        drawn = base * np.exp(spread * noise) if base else spread * noise
        out[name] = __import__('jax').numpy.asarray(drawn.astype(out[name].dtype))
    for name, factor in factors.items():
        out[name] = (out[name] * factor).astype(out[name].dtype)
    return out
```

```python
from contextlib import ExitStack

import concourse.bass as bass
from concourse import mybir

ALU = mybir.AluOpType
ACT = mybir.ActivationFunctionType
AX = mybir.AxisListType
F32 = mybir.dt.float32
F32R = mybir.dt.float32r
U32 = mybir.dt.uint32

P = 128
D = 1024
T = 512
KD = D // P
TC = T // P
HEADS = 8
HD = 64
PH = 8
TOPK = 16
NEG = -1e30
EPS = 1e-6
WINDOWS = (2, 4, 8, 16)
PAD = 16

N_IN, N_OUT, N_Q = 12, 8, 16
S_OUT = N_IN
S_Q = S_OUT + N_OUT
S_U = S_Q + N_Q
RING = 4
BT = 4
NBLK = P // BT
AHEAD = 2
STG = 64
NSTG = T // STG
GRP = 4
Y_BANK, ACC_BANK = 0, 4


def peer_block(nc, xT, w_qkp, w_v, w_pool, w_outq, w_uq, sub_keysT, expert_uT, expert_v, vecs, consts, outT):
    gates_dram = nc.dram_tensor("gates_dram", [NSTG, P, P * STG], F32, kind="Internal").ap()
    ctx = ExitStack()
    with ctx:
        def sem(name):
            return ctx.enter_context(nc.semaphore(name))

        base = (nc.sbuf_base + 63) // 64 * 64
        top = nc.sbuf_usable_end
        arena = ctx.enter_context(nc.sbuf_tensor("arena", [P, (top - base - 64) // 4], F32))

        def at(name, shape, dt, offset):
            n = 4
            for s in shape[1:]:
                n *= s
            n = (n + 31) // 32 * 32
            assert base + offset + n <= top - 64, (name, offset + n)
            return nc.alloc_sbuf_tensor_at(name, shape, dt, offset=base + offset), offset + n

        o = 0
        x1T, o = at("x1T", [P, KD, T], F32, o)
        act_hi, o = at("act_hi", [P, KD, T], F32R, o)
        act_lo, o = at("act_lo", [P, KD, T], F32R, o)
        w_raw, o = at("w_raw", [P, RING, KD, P], F32, o)
        w_hi, o = at("w_hi", [P, RING, KD, P], F32R, o)
        w_lo, o = at("w_lo", [P, RING, KD, P], F32R, o)
        ident, o = at("ident", [P, P], F32, o)
        iota, o = at("iota", [P, P], F32, o)
        vec_sb, o = at("vec_sb", [P, 3 * KD + 4], F32, o)
        ones, o = at("ones", [P, P], F32, o)
        eps_sb, o = at("eps_sb", [P, 8], F32, o)
        iT, o = at("iT", [P, T], F32, o)
        jT, o = at("jT", [P, T], F32, o)
        gT, o = at("gT", [P, T], F32, o)
        geluT, o = at("geluT", [P, AHEAD, BT, T], F32, o)
        R = o
        v_raw, o = at("v_raw", [P, 2, BT, T], F32, R)
        v_hi, o = at("v_hi", [P, BT, T], F32R, o)
        v_lo, o = at("v_lo", [P, BT, T], F32R, o)
        c_hi, o = at("c_hi", [P, 2, BT, T], F32R, o)
        c_lo, o = at("c_lo", [P, 2, BT, T], F32R, o)
        gate_in, o = at("gate_in", [P, 2, NSTG, BT, STG], F32, o)
        sq, o = at("sq", [P, KD, T], F32, R)
        std, o = at("std", [P, T], F32, o)
        var, o = at("var", [P, T], F32, o)
        rstd, o = at("rstd", [P, T], F32, o)
        tnw, o = at("tnw", [P, T], F32, o)
        rstd2, o = at("rstd2", [P, T], F32, o)
        RN = o
        qkT, o = at("qkT", [P, 8, T], F32, R)
        v_tok, o = at("v_tok", [P, TC, T], F32, RN)
        zp, o = at("zp", [P, 4, PAD + T], F32, o)
        cnt, o = at("cnt", [P, T], F32, o)
        negm, o = at("negm", [P, T], F32, o)
        rcw, o = at("rcw", [P, 4, PAD], F32, o)
        mx, o = at("mx", [P, 2, TC], F32, o)
        nb, o = at("nb", [P, 2, TC], F32, o)
        den, o = at("den", [P, 2, TC], F32, o)
        rden, o = at("rden", [P, 2, TC], F32, o)
        RM = o
        wv_raw, o = at("wv_raw", [P, 2, T], F32, RM)
        wv_hi, o = at("wv_hi", [P, 2, T], F32R, o)
        wv_lo, o = at("wv_lo", [P, 2, T], F32R, o)
        AW = 10 * P
        pr, o = at("pr", [P, 2, AW], F32, RM)
        pT, o = at("pT", [P, TC, T], F32, o)
        wpl, o = at("wpl", [P, 4, P], F32, o)
        assert RM - R >= 0
        lvl, _ = at("lvl", [P, 2, PAD + T], F32, R + 16 * 1024)
        ptmp, o = at("ptmp", [P, 4, T], F32, o)
        skT, o = at("skT", [P, 2 * PH, P], F32, RN)
        q2, o = at("q2", [P, 2, T], F32, o)
        topv, o = at("topv", [P, 2, TC, TOPK], F32, o)
        topi, o = at("topi", [P, 2, TC, TOPK], U32, o)
        tmp8, o = at("tmp8", [P, 2, P], F32, o)
        cand, o = at("cand", [P, TC, TOPK, TOPK], F32, o)
        tmpc, o = at("tmpc", [P, 2, TOPK * TOPK], F32, o)
        pos, o = at("pos", [P, TC, TOPK], U32, o)
        kk, o = at("kk", [P, 2, TC, TOPK], U32, o)
        best, o = at("best", [P, TC, PH, TOPK], F32, o)
        kf, o = at("kf", [P, 2, TC, PH, TOPK], F32, o)
        tf, o = at("tf", [P, 2, TC, PH, TOPK], F32, o)
        ij, o = at("ij", [P, 2, TC, PH, TOPK], F32, o)
        gsum, o = at("gsum", [P, TC, PH], F32, o)
        oh16, _ = at("oh16", [P, 2, PH, TOPK, TOPK], F32, R)
        stage, o = at("stage", [P, 2, P, STG], F32, R)
        oh_i, o = at("oh_i", [P, 2, GRP, P], F32, o)
        oh_g, o = at("oh_g", [P, 2, GRP, P], F32, o)

        ps = ctx.enter_context(nc.psum_tensor("ps", [P, 8, T], F32))

        x_in = sem("x_in")
        const_in = sem("const_in")
        w_in_sem = [sem(f"w_in{r}") for r in range(RING)]
        wv_in = [sem(f"wv_in{r}") for r in range(2)]
        pool_w_in = sem("pool_w_in")
        keys_in = sem("keys_in")
        v_in = [sem("v_in0"), sem("v_in1")]
        gate_in_sem = [sem("gate_in0"), sem("gate_in1")]
        stage_out = [sem("stage_out0"), sem("stage_out1")]
        out_done = sem("out_done")
        w_hi_done = sem("w_hi_done")
        w_lo_done = sem("w_lo_done")
        w_used = sem("w_used")
        acc_free = sem("acc_free")
        consts_set = sem("consts_set")
        sq_done = sem("sq_done")
        ssq_done = sem("ssq_done")
        std_done = sem("std_done")
        normed = sem("normed")
        act_hi_done = sem("act_hi_done")
        act_lo_done = sem("act_lo_done")
        wv_hi_done = sem("wv_hi_done")
        wv_lo_done = sem("wv_lo_done")
        wv_used = sem("wv_used")
        vtok_done = sem("vtok_done")
        s_done = sem("s_done")
        s_masked = sem("s_masked")
        nb_done = sem("nb_done")
        p_exp = sem("p_exp")
        p_cnt = sem("p_cnt")
        rden_done = sem("rden_done")
        p_norm = sem("p_norm")
        pt_done = sem("pt_done")
        pt_out = sem("pt_out")
        o_done = sem("o_done")
        o_hi = sem("o_hi")
        o_lo = sem("o_lo")
        sums_done = sem("sums_done")
        pooled_done = sem("pooled_done")
        pmix_done = sem("pmix_done")
        pscaled = sem("pscaled")
        pmix_hi = sem("pmix_hi")
        pmix_lo = sem("pmix_lo")
        sc_done = sem("sc_done")
        sc_used = sem("sc_used")
        ohk_done = sem("ohk_done")
        ohk_mul = sem("ohk_mul")
        ij_done = sem("ij_done")
        shifted = sem("shifted")
        g_exp = sem("g_exp")
        gates_done = sem("gates_done")
        tr_done = sem("tr_done")
        tr_out = sem("tr_out")
        oh_done = sem("oh_done")
        oh_used = sem("oh_used")
        gate_out = sem("gate_out")
        v_hi_done = sem("v_hi_done")
        v_lo_done = sem("v_lo_done")
        c_mul = sem("c_mul")
        c_hi_done = sem("c_hi_done")
        c_lo_done = sem("c_lo_done")
        y_done = sem("y_done")
        y_out = sem("y_out")
        dve_self = sem("dve_self")
        final_done = sem("final_done")

        block = ctx.enter_context(nc.Block())

        S_AT = ((0, 0), (1, 0), (0, P), (2, 0))
        P_AT = (0, P, 3 * P, 6 * P)

        def w_source(s):
            if s < S_OUT:
                return w_qkp[s]
            if s < S_Q:
                return w_outq[s - S_OUT]
            if s < S_U:
                return w_uq[s - S_Q]
            return expert_uT[s - S_U]

        @block.sync
        def _(sp):
            def load_w(s, src=None, first=False):
                if not first:
                    sp.wait_ge(w_lo_done, s - RING + 1)
                slot = s % RING if isinstance(s, int) else None
                sp.dma_start(w_raw[:, slot], w_source(s)).then_inc(w_in_sem[slot], 16)

            sp.dma_start(x1T[:], xT).then_inc(x_in, 16)
            sp.dma_start(vec_sb[:], vecs).then_inc(const_in, 16)
            sp.dma_start(ident[:], consts[:, 0:P]).then_inc(const_in, 16)
            sp.dma_start(iota[:], consts[:, P:2 * P]).then_inc(const_in, 16)
            sp.dma_start(cnt[:], consts[:, 2 * P:2 * P + T]).then_inc(const_in, 16)
            sp.dma_start(negm[:], consts[:, 2 * P + T:2 * P + 2 * T]).then_inc(const_in, 16)
            sp.dma_start(rcw[:], consts[:, 2 * P + 2 * T:2 * P + 2 * T + 4 * PAD].rearrange(
                "p (a b) -> p a b", a=4)).then_inc(const_in, 16)
            for s in range(RING):
                load_w(s, first=True)
            for s in range(RING, S_OUT + RING):
                load_w(s)
            for k in range(KD):
                if k >= 2:
                    sp.wait_ge(wv_lo_done, k - 1)
                sp.dma_start(wv_raw[:, k % 2], w_v[:, k]).then_inc(wv_in[k % 2], 16)
            sp.wait_ge(wv_used, KD)
            sp.dma_start(wpl[:], w_pool).then_inc(pool_w_in, 16)
            for s in range(S_OUT + RING, S_Q + RING):
                load_w(s)
            sp.wait_ge(o_lo, HEADS)
            sp.wait_ge(pmix_lo, 4)
            sp.dma_start(skT[:], sub_keysT).then_inc(keys_in, 16)
            for s in range(S_Q + RING, S_U + (AHEAD + 2) * BT):
                load_w(s)
            with sp.Fori(0, NSTG // 2) as c:
                for b in range(2):
                    sp.wait_ge(gate_out, (c * 2 + b + 1) * (STG // GRP))
                    sp.dma_start(gates_dram[bass.ds(c * 2 + b, 1)].rearrange("o p n -> (o p) n"),
                                 stage[:, b].rearrange("p j t -> p (j t)")).then_inc(stage_out[b], 16)
            for b in range(2):
                sp.wait_ge(stage_out[b], 16 * (NSTG // 2))

            def load_gates(n, par):
                src = gates_dram[:, :, bass.ds(n * (BT * STG), BT * STG)].rearrange(
                    "c i (j t) -> i c (j t)", t=STG)
                sp.dma_start(gate_in[:, par].rearrange("p c j t -> p c (j t)"), src).then_inc(gate_in_sem[par], 16)

            def load_v(n, half):
                src = expert_v.rearrange("(i j) d -> i j d", j=P)[:, bass.ds(n * BT, BT), half * T:(half + 1) * T]
                sp.dma_start(v_raw[:, half], src).then_inc(v_in[half], 16)

            def load_u(n, t):
                sp.wait_ge(w_lo_done, S_U + n * BT + t - RING + 1)
                sp.dma_start(w_raw[:, t], expert_uT[bass.ds(n * BT + t, 1)].rearrange(
                    "o p k m -> (o p) k m")).then_inc(w_in_sem[t], 16)

            load_gates(0, 0)
            load_v(0, 0)
            load_v(0, 1)
            load_gates(1, 1)

            def step(n, par, more):
                if more >= 2:
                    sp.wait_ge(c_mul, n + 1)
                    load_gates(n + 2, par)
                if more >= 1:
                    sp.wait_ge(v_lo_done, 2 * n + 1)
                    load_v(n + 1, 0)
                if more >= 4:
                    load_u(n + 4, 0)
                    load_u(n + 4, 1)
                if more >= 1:
                    sp.wait_ge(v_lo_done, 2 * n + 2)
                    load_v(n + 1, 1)
                if more >= 4:
                    load_u(n + 4, 2)
                    load_u(n + 4, 3)

            with sp.Fori(0, NBLK // 2 - 2) as i:
                for par in range(2):
                    step(i * 2 + par, par, NBLK)
            for n in range(NBLK - 4, NBLK):
                step(n, n % 2, NBLK - 1 - n)
            sp.wait_ge(final_done, KD)
            sp.dma_start(outT, sq[:]).then_inc(out_done, 16)
            sp.wait_ge(out_done, 16)

        @block.gpsimd
        def _(pool):
            pool.memset(ones[:], 1.0).then_inc(consts_set, 1)
            pool.memset(eps_sb[:], EPS).then_inc(consts_set, 1)
            pool.memset(zp[:, :, 0:PAD], 0.0).then_inc(consts_set, 1)

            def cut_lo(s, slot, checked=True):
                if checked:
                    pool.wait_ge(w_used, s - RING + 1)
                pool.wait_ge(w_hi_done, s + 1)
                pool.tensor_tensor(w_lo[:, slot], w_raw[:, slot], w_hi[:, slot].bitcast(F32),
                                   ALU.subtract).then_inc(w_lo_done, 1)

            for s in range(S_OUT + RING):
                cut_lo(s, s % RING, s >= RING)
            pool.wait_ge(acc_free, N_IN)
            pool.wait_ge(normed, KD)
            done = 0
            for g in range(4):
                src = zp[:, g]
                for l in range(g + 1):
                    w = 1 << l
                    lo = 2 * w - 1
                    if done:
                        pool.wait_ge(sums_done, done)
                    if l == 0 and g:
                        pool.wait_ge(pooled_done, 3 * g)
                    dst = lvl[:, l % 2]
                    pool.tensor_tensor(dst[:, lo:PAD + T], src[:, lo:PAD + T], src[:, lo - w:PAD + T - w],
                                       ALU.add).then_inc(sums_done, 1)
                    done += 1
                    src = dst
            for h in range(HEADS):
                pool.wait_ge(rden_done, h + 1)
                for i in range(TC):
                    a = pr[:, h % 2, P_AT[i]:P_AT[i] + (i + 1) * P]
                    pool.tensor_scalar(a, a, rden[:, h % 2, i:i + 1], None, ALU.mult).then_inc(p_norm, 1)
            for s in range(S_OUT + RING, S_U + (AHEAD + 1) * BT):
                cut_lo(s, s % RING)
            for n in range(2 * TC):
                w, tc = n % 2, n // 2
                pool.wait_ge(ohk_done, n + 1)
                pool.tensor_tensor(oh16[:, n % 2], oh16[:, n % 2],
                                   tf[:, w, tc].unsqueeze(2).broadcast_to([P, PH, TOPK, TOPK]),
                                   ALU.mult).then_inc(ohk_mul, 1)
            with pool.Fori(0, NBLK - AHEAD - 1) as n:
                for t in range(BT):
                    cut_lo(n * BT + (S_U + (AHEAD + 1) * BT + t), t)

        @block.scalar
        def _(act):
            def cut_hi(s, slot, uses):
                act.wait_ge(w_in_sem[slot], uses * 16)
                if not (isinstance(s, int) and s < RING):
                    act.wait_ge(w_used, s - RING + 1)
                act.activation(w_hi[:, slot], w_raw[:, slot], ACT.Copy).then_inc(w_hi_done, 1)

            def squares(n, done, count):
                act.wait_ge(done, count)
                for k in range(KD):
                    act.activation(sq[:, k], x1T[:, k], ACT.Square).then_inc(sq_done, 1)

            def root(n):
                act.wait_ge(ssq_done, n + 1)
                act.activation(std[:], ps[:, 6], ACT.Sqrt, scale=1.0 / D, bias=eps_sb[:, 0:1]).then_inc(std_done, 1)

            def high_of_normed(n):
                for k in range(KD):
                    act.wait_ge(normed, n * KD + k + 1)
                    act.activation(act_hi[:, k], sq[:, k], ACT.Copy).then_inc(act_hi_done, 1)

            act.wait_ge(consts_set, 3)
            squares(0, x_in, 16)
            for s in range(RING):
                cut_hi(s, s, 1)
            root(0)
            high_of_normed(0)
            for s in range(N_IN):
                act.wait_ge(w_used, s + 1)
                if s == 0:
                    act.wait_ge(act_lo_done, KD)
                out = qkT[:, s] if s < 8 else zp[:, s - 8, PAD:PAD + T]
                act.activation(out, ps[:, ACC_BANK + s % 2], ACT.Copy).then_inc(acc_free, 1)
                cut_hi(s + RING, (s + RING) % RING, (s + RING) // RING + 1)
            for k in range(KD):
                act.wait_ge(wv_in[k % 2], 16 * (k // 2 + 1))
                if k >= 2:
                    act.wait_ge(wv_used, k - 1)
                act.activation(wv_hi[:, k % 2], wv_raw[:, k % 2], ACT.Copy).then_inc(wv_hi_done, 1)
            act.wait_ge(wv_used, KD)
            for tc in range(TC):
                act.activation(v_tok[:, tc], ps[:, tc], ACT.Copy).then_inc(vtok_done, 1)

            def exps(h):
                act.wait_ge(nb_done, h + 1)
                for i in range(TC):
                    a = pr[:, h % 2, P_AT[i]:P_AT[i] + (i + 1) * P]
                    act.activation(a, a, ACT.Exp, scale=HD ** -0.5, bias=nb[:, h % 2, i:i + 1]).then_inc(p_exp, 1)

            def transposed_out(h):
                for i in range(TC):
                    act.wait_ge(pt_done, h * TC + i + 1)
                    if i == 0 and h:
                        act.wait_ge(o_done, h)
                    act.activation(pT[:, 0:i + 1, i * P:(i + 1) * P],
                                   ps[:, (3, 6)[i % 2], 0:(i + 1) * P].rearrange("p (a b) -> p a b", b=P),
                                   ACT.Copy).then_inc(pt_out, 1)
                act.wait_ge(o_done, h + 1)
                b = HD * (h % 2)
                act.activation(act_hi[b:b + HD, h // 2], ps[b:b + HD, 7], ACT.Copy).then_inc(o_hi, 1)

            for h in range(HEADS + 1):
                if h < HEADS:
                    exps(h)
                if h:
                    transposed_out(h - 1)
            for g in range(4):
                act.wait_ge(pscaled, g + 1)
                act.activation(act_hi[:, 4 + g], ptmp[:, g], ACT.Copy).then_inc(pmix_hi, 1)
            for s in range(S_OUT, S_Q):
                cut_hi(s + RING, (s + RING) % RING, (s + RING) // RING + 1)
            squares(1, acc_free, S_Q)
            root(1)
            act.wait_ge(w_used, S_Q)
            high_of_normed(1)
            for s in range(S_Q, S_U):
                act.wait_ge(w_used, s + 1)
                if s == S_Q:
                    act.wait_ge(act_lo_done, 2 * KD)
                if s >= S_Q + 2:
                    act.wait_ge(sc_done, s - S_Q - 1)
                act.activation(q2[:, s % 2], ps[:, ACC_BANK + s % 2], ACT.Copy).then_inc(acc_free, 1)
                cut_hi(s + RING, (s + RING) % RING, (s + RING) // RING + 1)
            for s in range(S_U, S_U + AHEAD * BT):
                act.wait_ge(w_used, s + 1)
                m = s - S_U
                act.activation(geluT[:, m // BT, m % BT], ps[:, ACC_BANK + s % 2], ACT.Gelu).then_inc(acc_free, 1)
                cut_hi(s + RING, (s + RING) % RING, (s + RING) // RING + 1)
            act.wait_ge(shifted, 1)
            act.activation(best[:], best[:], ACT.Exp).then_inc(g_exp, 1)
            act.wait_ge(tr_done, 1)
            act.activation(iT[:], ps[:, 0], ACT.Copy).then_inc(tr_out, 1)
            act.activation(jT[:], ps[:, 1], ACT.Copy).then_inc(tr_out, 1)
            act.activation(gT[:], ps[:, 2], ACT.Copy).then_inc(tr_out, 1)

            def gate_sums_out(b, c):
                if not isinstance(c, int):
                    act.wait_ge(stage_out[b], c * 16)
                with act.Fori(0, STG // GRP // 4) as g:
                    for u in range(4):
                        at4 = g * 4 + u
                        act.wait_ge(oh_used, (c * 2 + b) * (STG // GRP) + at4 + 1)
                        act.activation(
                            stage[:, b, :, bass.ds(at4 * GRP, GRP)].rearrange("p j t -> p t j"),
                            ps[:, u].rearrange("p (t j) -> p t j", j=P), ACT.Copy).then_inc(gate_out, 1)
            for b in range(2):
                gate_sums_out(b, 0)
            with act.Fori(1, NSTG // 2) as c:
                for b in range(2):
                    gate_sums_out(b, c)

            def cut_v(n, half):
                act.wait_ge(v_in[half], (n + 1) * 16)
                act.activation(v_hi[:], v_raw[:, half], ACT.Copy).then_inc(v_hi_done, 1)

            def cut_c(n, par, first=False):
                act.wait_ge(c_mul, n + 1)
                if not first:
                    pass
                act.activation(c_hi[:, par], geluT[:, par], ACT.Copy).then_inc(c_hi_done, 1)

            for b in range(2):
                act.wait_ge(stage_out[b], 16 * (NSTG // 2))
            cut_v(0, 0)
            cut_c(0, 0, True)

            def step(n, par, more):
                if more >= 1:
                    cut_c(n + 1, 1 - par)
                for half in range(2):
                    act.wait_ge(y_done, n * 8 + half * 4 + 4)
                    if half == 0:
                        cut_v(n, 1)
                    elif more >= 1:
                        cut_v(n + 1, 0)
                    for t in (2 * half, 2 * half + 1):
                        s = n * BT + (S_U + AHEAD * BT + t)
                        if more >= AHEAD:
                            act.wait_ge(w_used, s + 1)
                            if t == 0:
                                act.wait_ge(c_lo_done, n + 1)
                            act.activation(geluT[:, par, t], ps[:, ACC_BANK + t % 2],
                                           ACT.Gelu).then_inc(acc_free, 1)
                        if more >= AHEAD + 1:
                            cut_hi(s + BT, t, n + (S_U // RING + AHEAD + 2))

            with act.Fori(0, NBLK // 2 - 2) as i:
                for par in range(2):
                    step(i * 2 + par, par, NBLK)
            for n in range(NBLK - 4, NBLK):
                step(n, n % 2, NBLK - 1 - n)
            squares(2, y_out, NBLK * 8)
            root(2)

        @block.tensor
        def _(pe):
            def three(out, w, sl, m, start, stop):
                (wh, wl), (mh, ml) = w, m
                pe.matmul(out, wh[sl], mh, start=start, stop=False)
                pe.matmul(out, wh[sl], ml, start=False, stop=False)
                return pe.matmul(out, wl[sl], mh, start=False, stop=stop)

            def tile(s, slot, first=False):
                pe.wait_ge(w_lo_done, s + 1)
                if not first:
                    pe.wait_ge(acc_free, s - 1)
                for k in range(KD):
                    last = three(ps[:, ACC_BANK + slot % 2], (w_hi, w_lo), (slice(None), slot, k),
                                 (act_hi[:, k], act_lo[:, k]), k == 0, k == KD - 1)
                last.then_inc(w_used, 1)

            def sum_squares(n):
                for k in range(KD):
                    pe.wait_ge(sq_done, n * KD + k + 1)
                    last = pe.matmul(ps[:, 6], ones[:], sq[:, k], start=k == 0, stop=k == KD - 1)
                last.then_inc(ssq_done, 1)

            pe.wait_ge(const_in, 6 * 16)
            sum_squares(0)
            pe.wait_ge(act_lo_done, KD)
            for s in range(N_IN):
                tile(s, s % RING, s < 2)
            for k in range(KD):
                pe.wait_ge(wv_lo_done, k + 1)
                for tc in range(TC):
                    sl = slice(tc * P, (tc + 1) * P)
                    out = ps[:, tc]
                    pe.matmul(out, act_hi[:, k, sl], wv_hi[:, k % 2], start=k == 0, stop=False)
                    pe.matmul(out, act_lo[:, k, sl], wv_hi[:, k % 2], start=False, stop=False)
                    last = pe.matmul(out, act_hi[:, k, sl], wv_lo[:, k % 2], start=False, stop=k == KD - 1)
                last.then_inc(wv_used, 1)
            pe.wait_ge(vtok_done, TC)

            def scores(h):
                if h:
                    pe.wait_ge(s_masked, h * TC)
                b, c = HD * (h % 2), h // 2
                for i in range(TC):
                    bank, col = S_AT[i]
                    w = (i + 1) * P
                    pe.matmul(ps[:, bank, col:col + w], qkT[b:b + HD, c, i * P:(i + 1) * P],
                              qkT[b:b + HD, 4 + c, 0:w], start=True, stop=True).then_inc(s_done, 1)

            def weighted(h):
                for i in range(TC):
                    n = h * TC + i
                    pe.wait_ge(p_norm, n + 1)
                    if n >= 2:
                        pe.wait_ge(pt_out, n - 1)
                    for kb in range(i + 1):
                        a = P_AT[i] + kb * P
                        last = pe.transpose(ps[:, (3, 6)[i % 2], kb * P:(kb + 1) * P], pr[:, h % 2, a:a + P],
                                            ident[:])
                    last.then_inc(pt_done, 1)
                pe.wait_ge(pt_out, (h + 1) * TC)
                if h:
                    pe.wait_ge(o_lo, h)
                b = HD * (h % 2)
                for kb in range(TC):
                    last = pe.matmul(ps[b:b + HD, 7, kb * P:T], v_tok[:, kb, h * HD:(h + 1) * HD],
                                     pT[:, kb, kb * P:T], start=kb == 0, stop=kb == TC - 1)
                last.then_inc(o_done, 1)

            for h in range(HEADS + 1):
                if h < HEADS:
                    scores(h)
                if h:
                    weighted(h - 1)
            pe.wait_ge(pool_w_in, 16)
            for g in range(4):
                pe.wait_ge(pooled_done, 3 * g + 3)
                pe.matmul(ps[:, g], wpl[:, g], ptmp[:, g], start=True, stop=True).then_inc(pmix_done, 1)
            pe.wait_ge(o_lo, HEADS)
            pe.wait_ge(pmix_lo, 4)
            for s in range(S_OUT, S_Q):
                tile(s, s % RING)
            sum_squares(1)
            pe.wait_ge(act_lo_done, 2 * KD)
            pe.wait_ge(keys_in, 16)

            def key_scores(hp):
                pe.wait_ge(acc_free, S_Q + hp + 1)
                if hp >= 2:
                    pe.wait_ge(sc_used, hp - 1)
                for tc in range(TC):
                    last = pe.matmul(ps[:, 6 + hp % 2, tc * P:(tc + 1) * P], q2[:, hp % 2, tc * P:(tc + 1) * P],
                                     skT[:, hp], start=True, stop=True)
                last.then_inc(sc_done, 1)
                return last

            for hp in range(2 * PH + 1):
                if hp < 2 * PH:
                    tile(S_Q + hp, hp % RING)
                if hp:
                    key_scores(hp - 1)
            for s in range(S_U, S_U + AHEAD * BT):
                tile(s, s % RING)
            pe.wait_ge(ij_done, 2 * TC)
            pe.wait_ge(gates_done, 1)
            for w in range(3):
                for tc in range(TC):
                    src = (ij[:, w, tc] if w < 2 else best[:, tc]).rearrange("p h k -> p (h k)")
                    last = pe.transpose(ps[:, w, tc * P:(tc + 1) * P], src, ident[:])
            last.then_inc(tr_done, 1)
            pe.wait_ge(tr_out, 3)

            def gate_group(g, b, bank, again):
                pe.wait_ge(oh_done, g + 1)
                if again:
                    pe.wait_ge(gate_out, g - 3)
                for u in range(GRP):
                    last = pe.matmul(ps[:, bank, u * P:(u + 1) * P], oh_i[:, b, u], oh_g[:, b, u],
                                     start=True, stop=True)
                last.then_inc(oh_used, 1)
            for b in range(4):
                gate_group(b, b % 2, b, False)
            with pe.Fori(1, T // GRP // 4) as i:
                for b in range(4):
                    gate_group(i * 4 + b, b % 2, b, True)

            def combine(n, half, par, first=False):
                pe.wait_ge(v_lo_done, n * 2 + half + 1)
                if half == 0:
                    pe.wait_ge(c_lo_done, n + 1)
                for t in range(BT):
                    for m in range(4):
                        if t == 0 and not (first and half == 0):
                            pe.wait_ge(y_out, n * 8 + half * 4 + m - 3)
                        last = three(ps[:, Y_BANK + m], (v_hi, v_lo),
                                     (slice(None), t, slice(m * P, (m + 1) * P)),
                                     (c_hi[:, par, t], c_lo[:, par, t]), t == 0, t == BT - 1)
                        if t == BT - 1:
                            last.then_inc(y_done, 1)

            def step(n, par, more, first=False):
                for half in range(2):
                    combine(n, half, par, first)
                    if more >= AHEAD:
                        for t in (2 * half, 2 * half + 1):
                            tile(n * BT + (S_U + AHEAD * BT + t), t)

            pe.wait_ge(gate_out, T // GRP)
            step(0, 0, NBLK, True)
            step(1, 1, NBLK)
            with pe.Fori(1, NBLK // 2 - 1) as i:
                for par in range(2):
                    step(i * 2 + par, par, NBLK)
            for n in range(NBLK - 2, NBLK):
                step(n, n % 2, NBLK - 1 - n)
            sum_squares(2)

        @block.vector
        def _(dve):
            count = [0]

            def then(ins):
                count[0] += 1
                ins.then_inc(dve_self, 1)
                dve.wait_ge(dve_self, count[0])

            def norm(n):
                dve.wait_ge(std_done, n + 1)
                then(dve.reciprocal(rstd[:], std[:]))
                then(dve.tensor_scalar(var[:], ps[:, 6], 1.0 / D, EPS, ALU.mult, ALU.add))
                then(dve.tensor_tensor(tnw[:], rstd[:], rstd[:], ALU.mult))
                then(dve.tensor_tensor(tnw[:], tnw[:], var[:], ALU.mult))
                then(dve.tensor_scalar(tnw[:], tnw[:], -0.5, 1.5, ALU.mult, ALU.add))
                then(dve.tensor_tensor(rstd2[:], rstd[:], tnw[:], ALU.mult))
                for k in range(KD):
                    dve.scalar_tensor_tensor(sq[:, k], x1T[:, k], vec_sb[:, n * KD + k:n * KD + k + 1], rstd2[:],
                                             ALU.mult, ALU.mult).then_inc(normed if n < 2 else final_done, 1)

            def low_of_normed(n):
                for k in range(KD):
                    dve.wait_ge(act_hi_done, n * KD + k + 1)
                    dve.tensor_tensor(act_lo[:, k], sq[:, k], act_hi[:, k].bitcast(F32),
                                      ALU.subtract).then_inc(act_lo_done, 1)

            dve.wait_ge(const_in, 6 * 16)
            norm(0)
            low_of_normed(0)
            for k in range(KD):
                dve.wait_ge(wv_hi_done, k + 1)
                if k >= 2:
                    dve.wait_ge(wv_used, k - 1)
                dve.tensor_tensor(wv_lo[:, k % 2], wv_raw[:, k % 2], wv_hi[:, k % 2].bitcast(F32),
                                  ALU.subtract).then_inc(wv_lo_done, 1)
            dve.wait_ge(wv_used, KD)

            def mask(h):
                dve.wait_ge(s_done, (h + 1) * TC)
                if h >= 2:
                    dve.wait_ge(pt_done, (h - 1) * TC)
                for i in range(TC):
                    bank, col = S_AT[i]
                    w = (i + 1) * P
                    dve.tensor_tensor_reduce(pr[:, h % 2, P_AT[i]:P_AT[i] + w], ps[:, bank, col:col + w],
                                             negm[:, T - w:T], 1.0, -3e38, ALU.add, ALU.max,
                                             mx[:, h % 2, i:i + 1]).then_inc(s_masked, 1)
                dve.wait_ge(s_masked, (h + 1) * TC)
                dve.tensor_scalar(nb[:, h % 2], mx[:, h % 2], -(HD ** -0.5), None, ALU.mult).then_inc(nb_done, 1)

            def weigh(h):
                for i in range(TC):
                    dve.wait_ge(p_exp, h * TC + i + 1)
                    w = (i + 1) * P
                    a = pr[:, h % 2, P_AT[i]:P_AT[i] + w]
                    dve.tensor_tensor_reduce(a, a, cnt[:, T - w:T], 1.0, 0.0, ALU.mult, ALU.add,
                                             den[:, h % 2, i:i + 1]).then_inc(p_cnt, 1)
                dve.wait_ge(p_cnt, (h + 1) * TC)
                dve.reciprocal(rden[:, h % 2], den[:, h % 2]).then_inc(rden_done, 1)

            def low_of_head(h):
                dve.wait_ge(o_hi, h + 1)
                b = HD * (h % 2)
                dve.tensor_tensor(act_lo[b:b + HD, h // 2], ps[b:b + HD, 7], act_hi[b:b + HD, h // 2].bitcast(F32),
                                  ALU.subtract).then_inc(o_lo, 1)

            def pooled(g):
                dve.wait_ge(sums_done, (g + 1) * (g + 2) // 2)
                s, z = lvl[:, g % 2, PAD:], zp[:, g, PAD:]
                dve.scalar_tensor_tensor(ptmp[:, g, PAD:], s[:, PAD:], 1.0 / WINDOWS[g], z[:, PAD:], ALU.mult,
                                         ALU.subtract).then_inc(pooled_done, 1)
                dve.tensor_tensor(ptmp[:, g, 0:PAD], s[:, 0:PAD], rcw[:, g], ALU.mult).then_inc(pooled_done, 1)
                dve.wait_ge(pooled_done, 3 * g + 2)
                dve.tensor_tensor(ptmp[:, g, 0:PAD], ptmp[:, g, 0:PAD], z[:, 0:PAD],
                                  ALU.subtract).then_inc(pooled_done, 1)

            for g in range(4):
                pooled(g)
            mask(0)
            for h in range(HEADS):
                if h + 1 < HEADS:
                    mask(h + 1)
                weigh(h)
                if h:
                    low_of_head(h - 1)
            low_of_head(HEADS - 1)
            for g in range(4):
                dve.wait_ge(pmix_done, g + 1)
                dve.tensor_scalar(ptmp[:, g], ps[:, g], vec_sb[:, 3 * KD + g:3 * KD + g + 1], None,
                                  ALU.mult).then_inc(pscaled, 1)
            for g in range(4):
                dve.wait_ge(pmix_hi, g + 1)
                dve.tensor_tensor(act_lo[:, 4 + g], ptmp[:, g], act_hi[:, 4 + g].bitcast(F32),
                                  ALU.subtract).then_inc(pmix_lo, 1)
            for m in range(N_OUT):
                dve.wait_ge(w_used, S_OUT + m + 1)
                dve.tensor_tensor(x1T[:, m], ps[:, ACC_BANK + m % 2], x1T[:, m], ALU.add).then_inc(acc_free, 1)
            norm(1)
            low_of_normed(1)

            LOW = -3.4028235e38
            def top16(p, hp, tc):
                s = ps[:, 6 + p, tc * P:(tc + 1) * P]
                v, ix, t = topv[:, p, tc], topi[:, p, tc], tmp8[:, tc % 2]
                then(dve.max(v[:, 0:8], s))
                then(dve.match_replace(t, v[:, 0:8], s, LOW))
                then(dve.max(v[:, 8:16], t))
                dve.max_index(ix[:, 0:8], v[:, 0:8], s)
                then(dve.max_index(ix[:, 8:16], v[:, 8:16], t))

            for h in range(PH):
                for p in range(2):
                    hp = 2 * h + p
                    dve.wait_ge(sc_done, hp + 1)
                    for tc in range(TC):
                        top16(p, hp, tc)
                    dve.tensor_copy(tf[:, p, :, h], topi[:, p]).then_inc(sc_used, 1)
                then(dve.tensor_tensor(
                    cand[:], topv[:, 0].unsqueeze(3).broadcast_to([P, TC, TOPK, TOPK]),
                    topv[:, 1].unsqueeze(2).broadcast_to([P, TC, TOPK, TOPK]), ALU.add))
                for tc in range(TC):
                    c = cand[:, tc].rearrange("p a b -> p (a b)")
                    t = tmpc[:, tc % 2]
                    b = best[:, tc, h]
                    then(dve.max(b[:, 0:8], c))
                    then(dve.match_replace(t, b[:, 0:8], c, LOW))
                    then(dve.max(b[:, 8:16], t))
                    dve.max_index(pos[:, tc, 0:8], b[:, 0:8], c)
                    then(dve.max_index(pos[:, tc, 8:16], b[:, 8:16], t))
                dve.tensor_scalar(kk[:, 0], pos[:], 4, None, ALU.logical_shift_right)
                then(dve.tensor_scalar(kk[:, 1], pos[:], TOPK - 1, None, ALU.bitwise_and))
                for w in range(2):
                    then(dve.tensor_copy(kf[:, w, :, h], kk[:, w]))
            then(dve.tensor_copy(gsum[:], best[:, :, :, 0]))
            b3 = best[:].rearrange("p c h k -> p (c h) k")
            g3 = gsum[:].rearrange("p c h -> p (c h)").unsqueeze(2).broadcast_to([P, TC * PH, TOPK])
            dve.tensor_tensor(b3, b3, g3, ALU.subtract).then_inc(shifted, 1)

            def onehot16(n):
                w, tc = n % 2, n // 2
                if n >= 2:
                    dve.wait_ge(ij_done, n - 1)
                dve.tensor_tensor(
                    oh16[:, n % 2].rearrange("p h k m -> p (h k) m"),
                    kf[:, w, tc].rearrange("p h k -> p (h k)").unsqueeze(2).broadcast_to([P, PH * TOPK, TOPK]),
                    iota[:, 0:TOPK].unsqueeze(1).broadcast_to([P, PH * TOPK, TOPK]),
                    ALU.is_equal).then_inc(ohk_done, 1)

            def pick(n):
                w, tc = n % 2, n // 2
                dve.wait_ge(ohk_mul, n + 1)
                dve.tensor_reduce(ij[:, w, tc].rearrange("p h k -> p (h k)"),
                                  oh16[:, n % 2].rearrange("p h k m -> p (h k) m"), AX.X,
                                  ALU.add).then_inc(ij_done, 1)
            onehot16(0)
            for n in range(2 * TC):
                if n + 1 < 2 * TC:
                    onehot16(n + 1)
                pick(n)
            dve.wait_ge(g_exp, 1)
            then(dve.tensor_reduce(gsum[:].rearrange("p c h -> p (c h)"), b3, AX.X, ALU.add))
            then(dve.reciprocal(gsum[:], gsum[:]))
            dve.tensor_tensor(b3, b3, g3, ALU.mult).then_inc(gates_done, 1)
            dve.wait_ge(tr_out, 3)

            def columns(g, b, again):
                if again:
                    dve.wait_ge(oh_used, g - 1)
                for u in range(GRP):
                    t = bass.ds(g * GRP + u, 1)
                    dve.tensor_scalar(oh_i[:, b, u], iota[:], iT[:, t], None, ALU.is_equal)
                    last = dve.tensor_scalar(oh_g[:, b, u], iota[:], jT[:, t], gT[:, t], ALU.is_equal, ALU.mult)
                last.then_inc(oh_done, 1)
            for b in range(2):
                columns(b, b, False)
            with dve.Fori(1, T // GRP // 2) as i:
                for b in range(2):
                    columns(i * 2 + b, b, True)

            def gate_block(n, par, fill):
                dve.wait_ge(acc_free, n * BT + (S_U + BT))
                dve.wait_ge(gate_in_sem[par], fill * 16)
                c = geluT[:, par].rearrange("p j (c t) -> p j c t", t=STG)
                dve.tensor_tensor(c, c, gate_in[:, par].rearrange("p c j t -> p j c t"),
                                  ALU.mult).then_inc(c_mul, 1)

            def low_of_c(n, par):
                dve.wait_ge(c_hi_done, n + 1)
                dve.tensor_tensor(c_lo[:, par], geluT[:, par], c_hi[:, par].bitcast(F32),
                                  ALU.subtract).then_inc(c_lo_done, 1)

            def low_of_v(n, half):
                dve.wait_ge(v_hi_done, n * 2 + half + 1)
                dve.tensor_tensor(v_lo[:], v_raw[:, half], v_hi[:].bitcast(F32),
                                  ALU.subtract).then_inc(v_lo_done, 1)

            def add_out(n, half):
                for m in range(4):
                    dve.wait_ge(y_done, n * 8 + half * 4 + m + 1)
                    dve.tensor_tensor(x1T[:, half * 4 + m], ps[:, Y_BANK + m], x1T[:, half * 4 + m],
                                      ALU.add).then_inc(y_out, 1)

            for b in range(2):
                dve.wait_ge(stage_out[b], 16 * (NSTG // 2))
            low_of_v(0, 0)
            gate_block(0, 0, 1)
            low_of_c(0, 0)

            def step(n, par, fill, more):
                if more >= 1:
                    gate_block(n + 1, 1 - par, fill)
                    low_of_c(n + 1, 1 - par)
                add_out(n, 0)
                low_of_v(n, 1)
                add_out(n, 1)
                if more >= 1:
                    low_of_v(n + 1, 0)

            with dve.Fori(0, NBLK // 2 - 2) as i:
                for par in range(2):
                    step(i * 2 + par, par, i + (1 + par), NBLK)
            for n in range(NBLK - 4, NBLK):
                step(n, n % 2, (n + 1) // 2 + 1, NBLK - 1 - n)
            norm(2)


def kernel(x, norm_mix, w_in, w_pool, pool_scale, w_out, norm_ffn, w_query, sub_keys, expert_u, expert_v, norm_final):
    import numpy as np
    import concourse.bacc as bacc
    from concourse.bass_utils import run_bass_kernel_spmd

    f = np.ascontiguousarray
    tiles = lambda w, m: f(np.asarray(w).reshape(KD, P, m, P).transpose(2, 1, 0, 3))
    w_in = np.asarray(w_in)[0]
    qkp = np.concatenate([w_in[:, 0:1024], w_in[:, 1536:2048]], axis=1)
    col = lambda v, k: np.asarray(v).reshape(k, P).T
    vecs = f(np.concatenate([col(norm_mix, KD), col(norm_ffn, KD), col(norm_final, KD), col(pool_scale, 4)], axis=1))

    dist = np.arange(P)[:, None] + (T - P) - np.arange(T)[None, :]
    hold = np.zeros((P, T), np.float32)
    for window, dilation in ((128, 1), (512, 4), (2048, 16)):
        hold += ((dist >= 0) & (dist <= window) & (dist % dilation == 0)).astype(np.float32)
    rc = np.stack([1.0 / np.minimum(np.arange(1, PAD + 1), w) for w in WINDOWS]).astype(np.float32).reshape(1, -1)
    consts = f(np.concatenate([
        np.eye(P, dtype=np.float32), np.tile(np.arange(P, dtype=np.float32), (P, 1)), hold,
        np.where(hold > 0, 0.0, NEG).astype(np.float32), np.tile(rc, (P, 1))], axis=1))

    arrays = {
        "xT": f(np.asarray(x)[0].T.reshape(KD, P, T).transpose(1, 0, 2)),
        "w_qkp": tiles(qkp, N_IN),
        "w_v": f(w_in[:, 1024:1536].reshape(KD, P, T).transpose(1, 0, 2)),
        "w_pool": f(np.asarray(w_pool)[0].transpose(1, 0, 2)),
        "w_outq": tiles(np.asarray(w_out)[0], N_OUT),
        "w_uq": tiles(np.asarray(w_query)[0], N_Q),
        "sub_keysT": f(np.asarray(sub_keys)[0].reshape(2 * PH, P, P).transpose(2, 0, 1)),
        "expert_uT": f(np.asarray(expert_u)[0].reshape(P, P, KD, P).transpose(1, 3, 2, 0)),
        "expert_v": f(np.asarray(expert_v)[0]),
        "vecs": vecs,
        "consts": consts,
    }
    nc = bacc.Bacc("TRN2", target_bir_lowering=False, num_devices=1)
    aps = [nc.dram_tensor(n, a.shape, F32, kind="ExternalInput").ap() for n, a in arrays.items()]
    out = nc.dram_tensor("outT", (P, KD, T), F32, kind="ExternalOutput").ap()
    peer_block(nc, *aps, out)
    r = run_bass_kernel_spmd(nc, [arrays], core_ids=[0])
    y = np.asarray(r.results[0]["outT"])
    return f(y.transpose(1, 0, 2).reshape(D, T).T).reshape(1, T, D)
```

```python
from contextlib import ExitStack

import concourse.bass as bass
from concourse import mybir

ALU = mybir.AluOpType
ACT = mybir.ActivationFunctionType
AX = mybir.AxisListType
F32 = mybir.dt.float32
F32R = mybir.dt.float32r
U32 = mybir.dt.uint32

P = 128
D = 1024
T = 512
KD = D // P
TC = T // P
HEADS = 8
HD = 64
PH = 8
TOPK = 16
NEG = -1e30
EPS = 1e-6
WINDOWS = (2, 4, 8, 16)
PAD = 16

N_IN, N_OUT, N_Q = 12, 8, 16
S_OUT = N_IN
S_Q = S_OUT + N_OUT
B_PICK = 8
U_AMONG_Q = 16
U_BEHIND_Q = B_PICK * 4 - U_AMONG_Q
S_UQ = S_Q + N_Q + U_AMONG_Q
S_U = S_Q + N_Q
RING = 4
BT = 4
NBLK = P // BT
STG = 64
NSTG = T // STG
GRP = 4
SG = STG // GRP
AHEAD = 2
STORED = B_PICK + NSTG
TURNS_U = NBLK - STORED
LOOP_U = TURNS_U - 4
OUT_BANKS = 4
Y_BANK, ACC_BANK = 0, OUT_BANKS


def peer_block(nc, xT, w_qkp, w_v, w_pool, w_outq, w_uq, sub_keysT, expert_uT, expert_v, vecs, consts, outT):
    gates_dram = nc.dram_tensor("gates_dram", [NSTG, P, P * STG], F32, kind="Internal").ap()
    gelu_dram = nc.dram_tensor("gelu_dram", [STORED, P, BT * T], F32, kind="Internal").ap()
    ctx = ExitStack()
    with ctx:
        def sem(name):
            return ctx.enter_context(nc.semaphore(name))

        base = (nc.sbuf_base + 63) // 64 * 64
        top = nc.sbuf_usable_end
        arena = ctx.enter_context(nc.sbuf_tensor("arena", [P, (top - base - 64) // 4], F32))

        def at(name, shape, dt, offset):
            n = 4
            for s in shape[1:]:
                n *= s
            n = (n + 31) // 32 * 32
            assert base + offset + n <= top - 64, (name, offset + n)
            return nc.alloc_sbuf_tensor_at(name, shape, dt, offset=base + offset), offset + n

        o = 0
        x1T, o = at("x1T", [P, KD, T], F32, o)
        act_hi, o = at("act_hi", [P, KD, T], F32R, o)
        act_lo, o = at("act_lo", [P, KD, T], F32R, o)
        w_raw, o = at("w_raw", [P, RING, KD, P], F32, o)
        w_hi, o = at("w_hi", [P, RING, KD, P], F32R, o)
        v_hi2, _ = at("v_hi2", [P, BT, T], F32R, o - 4 * RING * KD * P)
        v_lo2, _ = at("v_lo2", [P, BT, T], F32R, o)
        w_lo, o = at("w_lo", [P, RING, KD, P], F32R, o)
        ident, o = at("ident", [P, P], F32, o)
        iota, o = at("iota", [P, P], F32, o)
        vec_sb, o = at("vec_sb", [P, 3 * KD + 4], F32, o)
        ones, o = at("ones", [P, P], F32, o)
        eps_sb, o = at("eps_sb", [P, 8], F32, o)
        iT, o = at("iT", [P, T], F32, o)
        jT, o = at("jT", [P, T], F32, o)
        gT, o = at("gT", [P, T], F32, o)
        pT, _ = at("pT", [P, 2, TC, T], F32, o)
        geluT, o = at("geluT", [P, AHEAD, BT, T], F32, o)
        R = o
        v_raw, o = at("v_raw", [P, 2, BT, T], F32, R)
        v_hi, o = at("v_hi", [P, BT, T], F32R, o)
        v_lo, o = at("v_lo", [P, BT, T], F32R, o)
        c_hi, o = at("c_hi", [P, 2, BT, T], F32R, o)
        c_lo, o = at("c_lo", [P, 2, BT, T], F32R, o)
        gate_in, o = at("gate_in", [P, 2, NSTG, BT, STG], F32, o)
        sq, o = at("sq", [P, KD, T], F32, R)
        std, o = at("std", [P, T], F32, o)
        var, o = at("var", [P, T], F32, o)
        rstd, o = at("rstd", [P, T], F32, o)
        tnw, o = at("tnw", [P, T], F32, o)
        rstd2, o = at("rstd2", [P, T], F32, o)
        RN = o
        qkT, o = at("qkT", [P, 8, T], F32, R)
        v_tok, o = at("v_tok", [P, TC, T], F32, RN)
        zp, o = at("zp", [P, 4, PAD + T], F32, o)
        cnt, o = at("cnt", [P, T], F32, o)
        negm, o = at("negm", [P, T], F32, o)
        rcw, o = at("rcw", [P, 4, PAD], F32, o)
        mx, o = at("mx", [P, 3, TC], F32, o)
        nb, o = at("nb", [P, 3, TC], F32, o)
        den, o = at("den", [P, 3, TC], F32, o)
        rden, o = at("rden", [P, 3, TC], F32, o)
        RM = o
        wv_raw, o = at("wv_raw", [P, 4, T], F32, RM)
        wv_hi, o = at("wv_hi", [P, 4, T], F32R, o)
        wv_lo, o = at("wv_lo", [P, 4, T], F32R, o)
        AW = 10 * P
        SLOTS = 3
        pr, o = at("pr", [P, SLOTS, AW], F32, RM)
        wpl, o = at("wpl", [P, 4, P], F32, o)
        lvl, _ = at("lvl", [P, 2, PAD + T], F32, R + 16 * 1024)
        ptmp, o = at("ptmp", [P, 4, T], F32, o)
        skT, o = at("skT", [P, 2 * PH, P], F32, RN)
        q2, o = at("q2", [P, 2, T], F32, o)
        topv, o = at("topv", [P, 2, TC, TOPK], F32, o)
        topi, o = at("topi", [P, 2, TC, TOPK], U32, o)
        tmp8, o = at("tmp8", [P, TC, P], F32, o)
        cand, o = at("cand", [P, TC, TOPK, TOPK], F32, o)
        tmpc, o = at("tmpc", [P, TC, TOPK * TOPK], F32, o)
        pos, o = at("pos", [P, TC, TOPK], U32, o)
        kk, o = at("kk", [P, 2, TC, TOPK], U32, o)
        best, o = at("best", [P, TC, PH, TOPK], F32, o)
        kf, o = at("kf", [P, 2, TC, PH, TOPK], F32, o)
        tf, o = at("tf", [P, 2, TC, PH, TOPK], F32, o)
        ij, o = at("ij", [P, 2, TC, PH, TOPK], F32, o)
        gsum, o = at("gsum", [P, TC, PH], F32, o)
        oh16, _ = at("oh16", [P, 2, PH, TOPK, TOPK], F32, R)
        stage, o = at("stage", [P, 2, P, STG], F32, R)
        oh_i, o = at("oh_i", [P, 4, GRP, P], F32, o)
        oh_g, o = at("oh_g", [P, 4, GRP, P], F32, o)

        ps = ctx.enter_context(nc.psum_tensor("ps", [P, 8, T], F32))

        x_in = [sem(f"x_in{q}") for q in range(4)]
        const_in = sem("const_in")
        w_in_sem = [sem(f"w_in{r}") for r in range(RING)]
        wv_in = [sem(f"wv_in{r}") for r in range(4)]
        pool_w_in = sem("pool_w_in")
        keys_in = sem("keys_in")
        v_in = [sem("v_in0"), sem("v_in1")]
        gate_in_sem = [sem("gate_in0"), sem("gate_in1")]
        gelu_out = [sem("gelu_out0"), sem("gelu_out1")]
        gelu_in = [sem("gelu_in0"), sem("gelu_in1")]
        stage_out = [sem("stage_out0"), sem("stage_out1")]
        out_done = sem("out_done")
        w_hi_done = sem("w_hi_done")
        w_lo_done = sem("w_lo_done")
        w_used = sem("w_used")
        acc_free = sem("acc_free")
        consts_set = sem("consts_set")
        sq_done = sem("sq_done")
        ssq_done = sem("ssq_done")
        std_done = sem("std_done")
        normed = sem("normed")
        act_hi_done = sem("act_hi_done")
        act_lo_done = sem("act_lo_done")
        wv_hi_done = sem("wv_hi_done")
        wv_lo_done = sem("wv_lo_done")
        wv_used = sem("wv_used")
        vtok_done = sem("vtok_done")
        s_done = sem("s_done")
        s_masked = sem("s_masked")
        nb_done = sem("nb_done")
        p_exp = sem("p_exp")
        p_cnt = sem("p_cnt")
        rden_done = sem("rden_done")
        p_norm = sem("p_norm")
        pt_done = sem("pt_done")
        pt_out = sem("pt_out")
        o_done = sem("o_done")
        o_hi = sem("o_hi")
        o_lo = sem("o_lo")
        sums_done = sem("sums_done")
        pooled_done = sem("pooled_done")
        pmix_done = sem("pmix_done")
        pscaled = sem("pscaled")
        pmix_hi = sem("pmix_hi")
        pmix_lo = sem("pmix_lo")
        sc_done = sem("sc_done")
        sc_used = sem("sc_used")
        cand_done = sem("cand_done")
        ohk_done = sem("ohk_done")
        ohk_mul = sem("ohk_mul")
        ij_done = sem("ij_done")
        shifted = sem("shifted")
        g_exp = sem("g_exp")
        gates_done = sem("gates_done")
        tr_done = sem("tr_done")
        tr_out = sem("tr_out")
        oh_done = sem("oh_done")
        oh_used = sem("oh_used")
        gate_out = sem("gate_out")
        v_hi_done = sem("v_hi_done")
        v_lo_done = sem("v_lo_done")
        c_mul = sem("c_mul")
        c_hi_done = sem("c_hi_done")
        c_lo_done = sem("c_lo_done")
        y_done = sem("y_done")
        y_out = sem("y_out")
        dve_self = sem("dve_self")
        final_done = sem("final_done")

        block = ctx.enter_context(nc.Block())

        S_AT = ((0, 0), (1, 0), (0, P), (2, 0))
        P_AT = (0, P, 3 * P, 6 * P)

        def w_source(s):
            if s < S_OUT:
                return w_qkp[s]
            if s < S_Q:
                return w_outq[s - S_OUT]
            if s < S_UQ:
                pair, r = divmod(s - S_Q, 4)
                return w_uq[2 * pair + r] if r < 2 else expert_uT[2 * pair + r - 2]
            return expert_uT[s - S_U]

        def last_of(block):
            return S_Q + 8 * block + 7 if block < U_AMONG_Q // BT else S_U + BT * block + BT - 1

        @block.sync
        def _(sp):
            def load_w(s, src=None, first=False):
                if not first:
                    sp.wait_ge(w_lo_done, s - RING + 1)
                slot = s % RING if isinstance(s, int) else None
                sp.dma_start(w_raw[:, slot], w_source(s)).then_inc(w_in_sem[slot], 16)

            for q in range(4):
                sp.dma_start(x1T[:, 2 * q:2 * q + 2], xT[:, 2 * q:2 * q + 2]).then_inc(x_in[q], 16)
            sp.dma_start(vec_sb[:], vecs).then_inc(const_in, 16)
            for s in range(RING):
                load_w(s, first=True)
            sp.dma_start(ident[:], consts[:, 0:P]).then_inc(const_in, 16)
            sp.dma_start(iota[:], consts[:, P:2 * P]).then_inc(const_in, 16)
            sp.dma_start(cnt[:], consts[:, 2 * P:2 * P + T]).then_inc(const_in, 16)
            sp.dma_start(negm[:], consts[:, 2 * P + T:2 * P + 2 * T]).then_inc(const_in, 16)
            sp.dma_start(rcw[:], consts[:, 2 * P + 2 * T:2 * P + 2 * T + 4 * PAD].rearrange(
                "p (a b) -> p a b", a=4)).then_inc(const_in, 16)
            for s in range(RING, S_OUT + RING):
                load_w(s)
            for k in range(KD):
                if k >= 4:
                    sp.wait_ge(wv_lo_done, k - 3)
                sp.dma_start(wv_raw[:, k % 4], w_v[:, k]).then_inc(wv_in[k % 4], 16)
            sp.wait_ge(wv_used, KD)
            sp.dma_start(wpl[:], w_pool).then_inc(pool_w_in, 16)
            for s in range(S_OUT + RING, S_Q + RING):
                load_w(s)
            sp.wait_ge(o_lo, HEADS)
            sp.wait_ge(pmix_lo, 4)
            sp.dma_start(skT[:], sub_keysT).then_inc(keys_in, 16)

            def store_gelu(block, par, last):
                sp.wait_ge(acc_free, last + 1)
                sp.dma_start(gelu_dram[bass.ds(block, 1)].rearrange("o p n -> (o p) n"),
                             geluT[:, par].rearrange("p j t -> p (j t)")).then_inc(gelu_out[par], 16)

            stores = {last_of(b) + RING + 1: b for b in range(B_PICK)}
            for s in range(S_Q + RING, S_U + (B_PICK + 2) * BT):
                load_w(s)
                if s in stores:
                    store_gelu(stores[s], stores[s] % 2, last_of(stores[s]))

            def load_u(n, t):
                sp.wait_ge(w_lo_done, S_U + n * BT + t - RING + 1)
                sp.dma_start(w_raw[:, t], expert_uT[bass.ds(n * BT + t, 1)].rearrange(
                    "o p k m -> (o p) k m")).then_inc(w_in_sem[t], 16)

            with sp.Fori(0, NSTG // 2) as i:
                for b in range(2):
                    c = i * 2 + b
                    for t in range(BT):
                        load_u(c + (B_PICK + 2), t)
                    store_gelu(c + B_PICK, b, c * BT + (S_U + B_PICK * BT + 3))
                    sp.wait_ge(gate_out, c * SG + (SG + OUT_BANKS))
                    sp.dma_start(gates_dram[bass.ds(c, 1)].rearrange("o p n -> (o p) n"),
                                 stage[:, b].rearrange("p j t -> p (j t)")).then_inc(stage_out[b], 16)

            def load_gates(n, par):
                src = gates_dram[:, :, bass.ds(n * (BT * STG), BT * STG)].rearrange(
                    "c i (j t) -> i c (j t)", t=STG)
                sp.dma_start(gate_in[:, par].rearrange("p c j t -> p c (j t)"), src).then_inc(gate_in_sem[par], 16)

            def load_gelu(n, par):
                sp.dma_start(geluT[:, par].rearrange("p j t -> p (j t)"),
                             gelu_dram[bass.ds(n, 1)].rearrange("o p n -> (o p) n")).then_inc(gelu_in[par], 16)

            def load_v(n, half):
                src = expert_v.rearrange("(i j) d -> i j d", j=P)[:, bass.ds(n * BT, BT), half * T:(half + 1) * T]
                sp.dma_start(v_raw[:, half], src).then_inc(v_in[half], 16)

            sp.wait_ge(stage_out[0], 16 * (NSTG // 2))
            load_v(STORED, 0)
            load_v(STORED, 1)
            for t in range(BT):
                load_u(STORED + 2, t)
            sp.wait_ge(stage_out[1], 16 * (NSTG // 2))
            load_gates(STORED, 0)
            load_gates(STORED + 1, 1)
            for t in range(BT):
                load_u(STORED + 3, t)
            for b in range(2):
                sp.wait_ge(gelu_out[b], 16 * (STORED // 2))

            def step(q, blk, par, nxt, nxt2, loads, stored=False):
                if nxt2 is not None:
                    sp.wait_ge(c_mul, q + 1)
                    load_gates(nxt2, par)
                    if stored:
                        sp.wait_ge(c_lo_done, q + 1)
                        load_gelu(nxt2, par)
                if nxt is not None:
                    sp.wait_ge(v_lo_done, q * 2 + 1)
                    load_v(nxt, 0)
                if loads:
                    load_u(blk + 4, 0)
                    load_u(blk + 4, 1)
                if nxt is not None:
                    sp.wait_ge(v_lo_done, q * 2 + 2)
                    load_v(nxt, 1)
                if loads:
                    load_u(blk + 4, 2)
                    load_u(blk + 4, 3)

            def block_of(q):
                return q + STORED if q < TURNS_U else q - TURNS_U

            with sp.Fori(0, LOOP_U // 2) as i:
                for par in range(2):
                    q = i * 2 + par
                    step(q, q + STORED, par, q + (STORED + 1), q + (STORED + 2), True)
            for q in range(LOOP_U, TURNS_U):
                step(q, block_of(q), q % 2, block_of(q + 1), block_of(q + 2), False, q + 2 >= TURNS_U)
            with sp.Fori(TURNS_U // 2, NBLK // 2 - 1) as i:
                for par in range(2):
                    q = i * 2 + par
                    b = (i - TURNS_U // 2) * 2 + par
                    step(q, b, par, b + 1, b + 2, False, True)
            for q in range(NBLK - 2, NBLK):
                step(q, block_of(q), q % 2, block_of(q + 1) if q + 1 < NBLK else None, None, False)
            for k in range(KD):
                sp.wait_ge(final_done, k + 1)
                sp.dma_start(outT[:, k], sq[:, k]).then_inc(out_done, 16)
            sp.wait_ge(out_done, KD * 16)

        @block.gpsimd
        def _(pool):
            pool.memset(ones[:], 1.0).then_inc(consts_set, 1)
            pool.memset(eps_sb[:], EPS).then_inc(consts_set, 1)
            pool.memset(zp[:, :, 0:PAD], 0.0).then_inc(consts_set, 1)

            def cut_lo(s, slot, checked=True):
                if checked:
                    pool.wait_ge(w_used, s - RING + 1)
                pool.wait_ge(w_hi_done, s + 1)
                pool.tensor_tensor(w_lo[:, slot], w_raw[:, slot], w_hi[:, slot].bitcast(F32),
                                   ALU.subtract).then_inc(w_lo_done, 1)

            for s in range(S_OUT + RING):
                cut_lo(s, s % RING, s >= RING)
            pool.wait_ge(acc_free, N_IN)
            pool.wait_ge(normed, KD)
            done = 0
            for g in range(4):
                src = zp[:, g]
                for l in range(g + 1):
                    w = 1 << l
                    lo = 2 * w - 1
                    if done:
                        pool.wait_ge(sums_done, done)
                    if l == 0 and g:
                        pool.wait_ge(pooled_done, 3 * g)
                    dst = lvl[:, l % 2]
                    pool.tensor_tensor(dst[:, lo:PAD + T], src[:, lo:PAD + T], src[:, lo - w:PAD + T - w],
                                       ALU.add).then_inc(sums_done, 1)
                    done += 1
                    src = dst
            for h in range(HEADS):
                pool.wait_ge(rden_done, h + 1)
                for i in range(TC):
                    a = pr[:, h % SLOTS, P_AT[i]:P_AT[i] + (i + 1) * P]
                    pool.tensor_scalar(a, a, rden[:, h % SLOTS, i:i + 1], None, ALU.mult).then_inc(p_norm, 1)
            for s in range(S_OUT + RING, S_UQ + RING):
                cut_lo(s, s % RING)
            for tc in range(TC):
                pool.wait_ge(ohk_done, tc + 1)
                pool.tensor_tensor(oh16[:, 0], oh16[:, 0], tf[:, 0, tc].unsqueeze(2).broadcast_to(
                    [P, PH, TOPK, TOPK]), ALU.mult).then_inc(ohk_mul, 1)
                for t in range(U_BEHIND_Q // TC):
                    s = S_UQ + RING + U_BEHIND_Q // TC * tc + t
                    cut_lo(s, s % RING)
            with pool.Fori(B_PICK + 1, NBLK) as n:
                for t in range(BT):
                    cut_lo(n * BT + (S_U + t), t)

        @block.scalar
        def _(act):
            def cut_hi(s, slot, uses):
                act.wait_ge(w_in_sem[slot], uses * 16)
                if not (isinstance(s, int) and s < RING):
                    act.wait_ge(w_used, s - RING + 1)
                act.activation(w_hi[:, slot], w_raw[:, slot], ACT.Copy).then_inc(w_hi_done, 1)

            def square(k):
                act.activation(sq[:, k], x1T[:, k], ACT.Square).then_inc(sq_done, 1)

            def root(n):
                act.wait_ge(ssq_done, n + 1)
                act.activation(std[:], ps[:, 6], ACT.Sqrt, scale=1.0 / D, bias=eps_sb[:, 0:1]).then_inc(std_done, 1)

            def high_of_normed(n):
                for k in range(KD):
                    act.wait_ge(normed, n * KD + k + 1)
                    act.activation(act_hi[:, k], sq[:, k], ACT.Copy).then_inc(act_hi_done, 1)

            act.wait_ge(consts_set, 3)
            for k in range(KD):
                act.wait_ge(x_in[k // 2], 16)
                square(k)
            for s in range(RING):
                cut_hi(s, s, 1)
            root(0)
            high_of_normed(0)
            for s in range(N_IN):
                act.wait_ge(w_used, s + 1)
                if s == 0:
                    act.wait_ge(act_lo_done, KD)
                out = qkT[:, s] if s < 8 else zp[:, s - 8, PAD:PAD + T]
                act.activation(out, ps[:, ACC_BANK + s % 2], ACT.Copy).then_inc(acc_free, 1)
                cut_hi(s + RING, (s + RING) % RING, (s + RING) // RING + 1)
            for k in range(KD):
                act.wait_ge(wv_in[k % 4], 16 * (k // 4 + 1))
                if k >= 4:
                    act.wait_ge(wv_used, k - 3)
                act.activation(wv_hi[:, k % 4], wv_raw[:, k % 4], ACT.Copy).then_inc(wv_hi_done, 1)
            act.wait_ge(wv_used, KD)
            for tc in range(TC):
                act.activation(v_tok[:, tc], ps[:, tc], ACT.Copy).then_inc(vtok_done, 1)

            def exps(h):
                act.wait_ge(nb_done, h + 1)
                for i in range(TC):
                    a = pr[:, h % SLOTS, P_AT[i]:P_AT[i] + (i + 1) * P]
                    act.activation(a, a, ACT.Exp, scale=HD ** -0.5, bias=nb[:, h % SLOTS, i:i + 1]).then_inc(p_exp, 1)

            def transposed_out(h):
                for i in range(TC):
                    act.wait_ge(pt_done, h * TC + i + 1)
                    if i == 0 and h >= 2:
                        act.wait_ge(o_done, h - 1)
                    act.activation(pT[:, h % 2, 0:i + 1, i * P:(i + 1) * P],
                                   ps[:, (3, 6)[i % 2], 0:(i + 1) * P].rearrange("p (a b) -> p a b", b=P),
                                   ACT.Copy).then_inc(pt_out, 1)

            def head_out(h):
                act.wait_ge(o_done, h + 1)
                b = HD * (h % 2)
                act.activation(act_hi[b:b + HD, h // 2], ps[b:b + HD, 7], ACT.Copy).then_inc(o_hi, 1)

            for h in range(HEADS + 3):
                if 2 <= h < HEADS + 2:
                    transposed_out(h - 2)
                if h >= 3:
                    head_out(h - 3)
                if h < HEADS:
                    exps(h)
            for g in range(4):
                act.wait_ge(pscaled, g + 1)
                act.activation(act_hi[:, 4 + g], ptmp[:, g], ACT.Copy).then_inc(pmix_hi, 1)
            for s in range(S_OUT, S_Q):
                if s >= S_OUT + 2:
                    act.wait_ge(acc_free, s - 1)
                    square(s - 2 - S_OUT)
                cut_hi(s + RING, (s + RING) % RING, (s + RING) // RING + 1)
            for k in (KD - 2, KD - 1):
                act.wait_ge(acc_free, S_OUT + k + 1)
                square(k)
            root(1)
            act.wait_ge(w_used, S_Q)
            high_of_normed(1)

            def gelu(u, slot, s, free=None):
                act.wait_ge(w_used, s + 1)
                if free is not None:
                    act.wait_ge(gelu_out[slot], free)
                act.activation(geluT[:, slot, u], ps[:, ACC_BANK + u % 2], ACT.Gelu).then_inc(acc_free, 1)

            for s in range(S_Q, S_UQ + (B_PICK * BT - U_AMONG_Q)):
                pair, part = divmod(s - S_Q, 4)
                if s < S_UQ and part < 2:
                    hp = 2 * pair + part
                    act.wait_ge(w_used, s + 1)
                    if hp >= 2:
                        act.wait_ge(sc_done, hp - 1)
                    act.activation(q2[:, hp % 2], ps[:, ACC_BANK + s % 2], ACT.Copy).then_inc(acc_free, 1)
                else:
                    u = 2 * pair + part - 2 if s < S_UQ else s - S_U
                    blk = u // BT
                    gelu(u % BT, blk % 2, s, 16 * (blk // 2) if u % BT == 0 and blk >= 2 else None)
                cut_hi(s + RING, (s + RING) % RING, (s + RING) // RING + 1)
            act.wait_ge(shifted, 1)
            act.activation(best[:], best[:], ACT.Exp).then_inc(g_exp, 1)
            act.wait_ge(tr_done, 1)
            act.activation(iT[:], ps[:, 0], ACT.Copy).then_inc(tr_out, 1)
            act.activation(jT[:], ps[:, 1], ACT.Copy).then_inc(tr_out, 1)
            act.activation(gT[:], ps[:, 2], ACT.Copy).then_inc(tr_out, 1)
            act.wait_ge(tr_out, 3)
            act.nop().then_inc(gate_out, OUT_BANKS)

            def gate_sums_out(c, b, first):
                if not first:
                    act.wait_ge(stage_out[b], 16 * (c // 2) if isinstance(c, int) else c_half[0] * 16)
                for g in range(SG):
                    act.wait_ge(oh_used, c * SG + (g + 1))
                    act.activation(stage[:, b, :, g * GRP:(g + 1) * GRP].rearrange("p j t -> p t j"),
                                   ps[:, g % 4].rearrange("p (t j) -> p t j", j=P), ACT.Copy).then_inc(gate_out, 1)
                    if g % 4 == 3:
                        t = g // 4
                        s = c * BT + (S_U + B_PICK * BT + t)
                        half = c // 2 if isinstance(c, int) else c_half[0]
                        gelu(t, b, s, (half + B_PICK // 2) * 16 if t == 0 else None)
                        cut_hi(s + BT, t, c + (S_U // RING + B_PICK + 2))

            c_half = [None]
            gate_sums_out(0, 0, True)
            gate_sums_out(1, 1, True)
            with act.Fori(1, NSTG // 2) as i:
                c_half[0] = i
                for b in range(2):
                    gate_sums_out(i * 2 + b, b, False)

            def cut_v(n, half):
                act.wait_ge(v_in[half], (n + 1) * 16)
                act.activation(v_hi[:], v_raw[:, half], ACT.Copy).then_inc(v_hi_done, 1)

            def cut_c(n, par):
                act.wait_ge(c_mul, n + 1)
                act.activation(c_hi[:, par], geluT[:, par], ACT.Copy).then_inc(c_hi_done, 1)

            def cut_v2(q):
                act.wait_ge(v_in[1], (q + 1) * 16)
                act.activation(v_hi2[:], v_raw[:, 1], ACT.Copy).then_inc(v_hi_done, 1)

            def tiles_between(q, half, cut):
                for t in (2 * half, 2 * half + 1):
                    s = q * BT + (S_U + (STORED + AHEAD) * BT + t)
                    if t == 0:
                        act.wait_ge(c_lo_done, q + 1)
                    gelu(t, par_of[0], s)
                    if cut:
                        cut_hi(s + BT, t, q + (S_U // RING + STORED + AHEAD + 2))

            for blk in (STORED, STORED + 1):
                for t in range(BT):
                    s = S_U + blk * BT + t
                    gelu(t, blk % 2, s, 16 * (blk // 2) if t == 0 else None)
                    cut_hi(s + BT, t, (s + BT) // RING + 1)
                if blk == STORED:
                    act.wait_ge(stage_out[0], 16 * (NSTG // 2))
                    cut_v(0, 0)
            act.wait_ge(stage_out[1], 16 * (NSTG // 2))
            cut_c(0, 0)
            par_of = [0]

            def step(q, par, cut):
                par_of[0] = par
                cut_c(q + 1, 1 - par)
                act.wait_ge(y_done, q * 8 + 4)
                cut_v(q, 1)
                tiles_between(q, 0, cut)
                act.wait_ge(y_done, q * 8 + 8)
                cut_v(q + 1, 0)
                tiles_between(q, 1, cut)

            with act.Fori(0, LOOP_U // 2) as i:
                for par in range(2):
                    step(i * 2 + par, par, True)
            for q in range(LOOP_U, TURNS_U - AHEAD):
                step(q, q % 2, q + AHEAD + 1 < TURNS_U)

            def stored_step(q, par, last):
                cut_v2(q)
                if not last:
                    cut_c(q + 1, 1 - par)
                act.wait_ge(y_done, q * 8 + 4)
                if not last:
                    cut_v(q + 1, 0)
                    act.wait_ge(y_done, q * 8 + 8)

            with act.Fori((TURNS_U - AHEAD) // 2, NBLK // 2 - 1) as i:
                for par in range(2):
                    stored_step(i * 2 + par, par, False)
            stored_step(NBLK - 2, 0, False)
            stored_step(NBLK - 1, 1, True)
            for k in range(KD):
                act.wait_ge(y_out, OUT_BANKS + (NBLK - 1) * 8 + k + 1)
                square(k)
            root(2)

        @block.tensor
        def _(pe):
            def three(out, w, sl, m, start, stop):
                (wh, wl), (mh, ml) = w, m
                pe.matmul(out, wh[sl], mh, start=start, stop=False)
                pe.matmul(out, wh[sl], ml, start=False, stop=False)
                return pe.matmul(out, wl[sl], mh, start=False, stop=stop)

            def tile(s, slot, first=False, part=range(KD), act_ready=None):
                if part[0] == 0:
                    pe.wait_ge(w_lo_done, s + 1)
                    if not first:
                        pe.wait_ge(acc_free, s - 1)
                for k in part:
                    if act_ready is not None:
                        pe.wait_ge(act_lo_done, act_ready + k + 1)
                    last = three(ps[:, ACC_BANK + slot % 2], (w_hi, w_lo), (slice(None), slot, k),
                                 (act_hi[:, k], act_lo[:, k]), k == 0, k == KD - 1)
                if part[-1] == KD - 1:
                    last.then_inc(w_used, 1)

            def sum_squares(n):
                for k in range(KD):
                    pe.wait_ge(sq_done, n * KD + k + 1)
                    last = pe.matmul(ps[:, 6], ones[:], sq[:, k], start=k == 0, stop=k == KD - 1)
                last.then_inc(ssq_done, 1)

            pe.wait_ge(consts_set, 3)
            sum_squares(0)
            for s in range(N_IN):
                tile(s, s % RING, s < 2, act_ready=None if s else 0)
            for k in range(KD):
                pe.wait_ge(wv_lo_done, k + 1)
                for tc in range(TC):
                    sl = slice(tc * P, (tc + 1) * P)
                    out = ps[:, tc]
                    pe.matmul(out, act_hi[:, k, sl], wv_hi[:, k % 4], start=k == 0, stop=False)
                    pe.matmul(out, act_lo[:, k, sl], wv_hi[:, k % 4], start=False, stop=False)
                    last = pe.matmul(out, act_hi[:, k, sl], wv_lo[:, k % 4], start=False, stop=k == KD - 1)
                last.then_inc(wv_used, 1)
            pe.wait_ge(vtok_done, TC)

            def scores(h):
                if h:
                    pe.wait_ge(s_masked, h * TC)
                b, c = HD * (h % 2), h // 2
                for i in range(TC):
                    bank, col = S_AT[i]
                    w = (i + 1) * P
                    pe.matmul(ps[:, bank, col:col + w], qkT[b:b + HD, c, i * P:(i + 1) * P],
                              qkT[b:b + HD, 4 + c, 0:w], start=True, stop=True).then_inc(s_done, 1)

            def transposes(h):
                if h == 0:
                    pe.wait_ge(const_in, 6 * 16)
                for i in range(TC):
                    n = h * TC + i
                    pe.wait_ge(p_norm, n + 1)
                    if n >= 2:
                        pe.wait_ge(pt_out, n - 1)
                    for kb in range(i + 1):
                        a = P_AT[i] + kb * P
                        last = pe.transpose(ps[:, (3, 6)[i % 2], kb * P:(kb + 1) * P], pr[:, h % SLOTS, a:a + P],
                                            ident[:])
                    last.then_inc(pt_done, 1)

            def weighted(h):
                pe.wait_ge(pt_out, (h + 1) * TC)
                if h:
                    pe.wait_ge(o_lo, h)
                b = HD * (h % 2)
                for kb in range(TC):
                    last = pe.matmul(ps[b:b + HD, 7, kb * P:T], v_tok[:, kb, h * HD:(h + 1) * HD],
                                     pT[:, h % 2, kb, kb * P:T], start=kb == 0, stop=kb == TC - 1)
                last.then_inc(o_done, 1)

            for h in range(HEADS + 3):
                if h < HEADS:
                    scores(h)
                if 2 <= h < HEADS + 2:
                    transposes(h - 2)
                if h >= 3:
                    weighted(h - 3)
            pe.wait_ge(pool_w_in, 16)
            for g in range(4):
                pe.wait_ge(pooled_done, 3 * g + 3)
                pe.matmul(ps[:, g], wpl[:, g], ptmp[:, g], start=True, stop=True).then_inc(pmix_done, 1)
            pe.wait_ge(o_lo, HEADS)
            pe.wait_ge(pmix_lo, 4)
            for s in range(S_OUT, S_Q):
                tile(s, s % RING)
            sum_squares(1)

            def key_scores(hp):
                if hp == 0:
                    pe.wait_ge(keys_in, 16)
                s = S_Q + 4 * (hp // 2) + hp % 2
                pe.wait_ge(acc_free, s + 1)
                if hp >= 2:
                    pe.wait_ge(sc_used, hp - 1)
                for tc in range(TC):
                    last = pe.matmul(ps[:, 6 + hp % 2, tc * P:(tc + 1) * P], q2[:, hp % 2, tc * P:(tc + 1) * P],
                                     skT[:, hp], start=True, stop=True)
                last.then_inc(sc_done, 1)
                return last

            for s in range(S_Q, S_UQ):
                tile(s, s % RING, act_ready=None if s > S_Q else KD)
                pair, part = divmod(s - S_Q, 4)
                if part in (1, 2):
                    key_scores(2 * pair + part - 1)
            for s in range(S_UQ, S_U + B_PICK * BT):
                tile(s, s % RING)
            pe.wait_ge(ij_done, 2 * TC)
            pe.wait_ge(gates_done, 1)
            for w in range(3):
                for tc in range(TC):
                    src = (ij[:, w, tc] if w < 2 else best[:, tc]).rearrange("p h k -> p (h k)")
                    last = pe.transpose(ps[:, w, tc * P:(tc + 1) * P], src, ident[:])
            last.then_inc(tr_done, 1)

            def gate_group(g, slot):
                pe.wait_ge(oh_done, g + 1)
                pe.wait_ge(gate_out, g + 1)
                for u in range(GRP):
                    last = pe.matmul(ps[:, slot, u * P:(u + 1) * P], oh_i[:, slot, u], oh_g[:, slot, u],
                                     start=True, stop=True)
                last.then_inc(oh_used, 1)

            with pe.Fori(0, NSTG) as c:
                for pair in range(SG // 2):
                    for b in range(2):
                        gate_group(c * SG + (2 * pair + b), (2 * pair + b) % 4)
                    t, half = divmod(pair, 2)
                    tile(c * BT + (S_U + B_PICK * BT + t), t, part=range(half * KD // 2, (half + 1) * KD // 2))
            for s in range(S_U + STORED * BT, S_U + (STORED + AHEAD) * BT):
                tile(s, s % RING)

            def combine(q, half, par, v):
                pe.wait_ge(v_lo_done, q * 2 + half + 1)
                if half == 0:
                    pe.wait_ge(c_lo_done, q + 1)
                for t in range(BT):
                    for m in range(OUT_BANKS):
                        if t == 0:
                            pe.wait_ge(y_out, q * 8 + (half * OUT_BANKS + m + 1))
                        last = three(ps[:, Y_BANK + m], v, (slice(None), t, slice(m * P, (m + 1) * P)),
                                     (c_hi[:, par, t], c_lo[:, par, t]), t == 0, t == BT - 1)
                        if t == BT - 1:
                            last.then_inc(y_done, 1)

            def step(q, par):
                for half in range(2):
                    combine(q, half, par, (v_hi, v_lo))
                    for t in (2 * half, 2 * half + 1):
                        tile(q * BT + (S_U + (STORED + AHEAD) * BT + t), t)

            with pe.Fori(0, (TURNS_U - AHEAD) // 2) as i:
                for par in range(2):
                    step(i * 2 + par, par)
            with pe.Fori((TURNS_U - AHEAD) // 2, NBLK // 2) as i:
                for par in range(2):
                    q = i * 2 + par
                    combine(q, 0, par, (v_hi, v_lo))
                    combine(q, 1, par, (v_hi2, v_lo2))
            sum_squares(2)

        @block.vector
        def _(dve):
            count = [0]

            def then(ins):
                count[0] += 1
                ins.then_inc(dve_self, 1)
                dve.wait_ge(dve_self, count[0])

            def norm(n):
                dve.wait_ge(std_done, n + 1)
                dve.tensor_scalar(var[:], ps[:, 6], 1.0 / D, EPS, ALU.mult, ALU.add)
                then(dve.reciprocal(rstd[:], std[:]))
                then(dve.tensor_tensor(tnw[:], rstd[:], rstd[:], ALU.mult))
                then(dve.tensor_tensor(tnw[:], tnw[:], var[:], ALU.mult))
                then(dve.tensor_scalar(tnw[:], tnw[:], -0.5, 1.5, ALU.mult, ALU.add))
                then(dve.tensor_tensor(rstd2[:], rstd[:], tnw[:], ALU.mult))
                for k in range(KD + 2):
                    if k < KD:
                        dve.scalar_tensor_tensor(
                            sq[:, k], x1T[:, k], vec_sb[:, n * KD + k:n * KD + k + 1], rstd2[:],
                            ALU.mult, ALU.mult).then_inc(normed if n < 2 else final_done, 1)
                    if k >= 2 and n < 2:
                        dve.wait_ge(act_hi_done, n * KD + k - 1)
                        dve.tensor_tensor(act_lo[:, k - 2], sq[:, k - 2], act_hi[:, k - 2].bitcast(F32),
                                          ALU.subtract).then_inc(act_lo_done, 1)

            dve.wait_ge(const_in, 6 * 16)
            norm(0)
            for k in range(KD):
                dve.wait_ge(wv_hi_done, k + 1)
                if k >= 4:
                    dve.wait_ge(wv_used, k - 3)
                dve.tensor_tensor(wv_lo[:, k % 4], wv_raw[:, k % 4], wv_hi[:, k % 4].bitcast(F32),
                                  ALU.subtract).then_inc(wv_lo_done, 1)
            dve.wait_ge(wv_used, KD)

            def mask(h):
                dve.wait_ge(s_done, (h + 1) * TC)
                if h >= SLOTS:
                    dve.wait_ge(pt_done, (h - SLOTS + 1) * TC)
                for i in range(TC):
                    bank, col = S_AT[i]
                    w = (i + 1) * P
                    dve.tensor_tensor_reduce(pr[:, h % SLOTS, P_AT[i]:P_AT[i] + w], ps[:, bank, col:col + w],
                                             negm[:, T - w:T], 1.0, -3e38, ALU.add, ALU.max,
                                             mx[:, h % SLOTS, i:i + 1]).then_inc(s_masked, 1)
                dve.wait_ge(s_masked, (h + 1) * TC)
                dve.tensor_scalar(nb[:, h % SLOTS], mx[:, h % SLOTS], -(HD ** -0.5), None, ALU.mult).then_inc(nb_done, 1)

            def weigh(h):
                for i in range(TC):
                    dve.wait_ge(p_exp, h * TC + i + 1)
                    w = (i + 1) * P
                    a = pr[:, h % SLOTS, P_AT[i]:P_AT[i] + w]
                    dve.tensor_tensor_reduce(a, a, cnt[:, T - w:T], 1.0, 0.0, ALU.mult, ALU.add,
                                             den[:, h % SLOTS, i:i + 1]).then_inc(p_cnt, 1)
                dve.wait_ge(p_cnt, (h + 1) * TC)
                dve.reciprocal(rden[:, h % SLOTS], den[:, h % SLOTS]).then_inc(rden_done, 1)

            def low_of_head(h):
                dve.wait_ge(o_hi, h + 1)
                b = HD * (h % 2)
                dve.tensor_tensor(act_lo[b:b + HD, h // 2], ps[b:b + HD, 7], act_hi[b:b + HD, h // 2].bitcast(F32),
                                  ALU.subtract).then_inc(o_lo, 1)

            def pooled(g):
                dve.wait_ge(sums_done, (g + 1) * (g + 2) // 2)
                s, z = lvl[:, g % 2, PAD:], zp[:, g, PAD:]
                dve.scalar_tensor_tensor(ptmp[:, g, PAD:], s[:, PAD:], 1.0 / WINDOWS[g], z[:, PAD:], ALU.mult,
                                         ALU.subtract).then_inc(pooled_done, 1)
                dve.tensor_tensor(ptmp[:, g, 0:PAD], s[:, 0:PAD], rcw[:, g], ALU.mult).then_inc(pooled_done, 1)
                dve.wait_ge(pooled_done, 3 * g + 2)
                dve.tensor_tensor(ptmp[:, g, 0:PAD], ptmp[:, g, 0:PAD], z[:, 0:PAD],
                                  ALU.subtract).then_inc(pooled_done, 1)

            for g in range(4):
                pooled(g)
            for h in range(HEADS + 4):
                if h < HEADS:
                    mask(h)
                if 1 <= h <= HEADS:
                    weigh(h - 1)
                if h >= 4:
                    low_of_head(h - 4)
            for g in range(4):
                dve.wait_ge(pmix_done, g + 1)
                dve.tensor_scalar(ptmp[:, g], ps[:, g], vec_sb[:, 3 * KD + g:3 * KD + g + 1], None,
                                  ALU.mult).then_inc(pscaled, 1)
            for g in range(4):
                dve.wait_ge(pmix_hi, g + 1)
                dve.tensor_tensor(act_lo[:, 4 + g], ptmp[:, g], act_hi[:, 4 + g].bitcast(F32),
                                  ALU.subtract).then_inc(pmix_lo, 1)
            for m in range(N_OUT):
                dve.wait_ge(w_used, S_OUT + m + 1)
                dve.tensor_tensor(x1T[:, m], ps[:, ACC_BANK + m % 2], x1T[:, m], ALU.add).then_inc(acc_free, 1)
            norm(1)

            LOW = -3.4028235e38
            def sixteen_best(n, values, index, source, spare):
                for stage in range(4):
                    for c in range(n):
                        v, ix, s, t = values(c), index(c), source(c), spare(c)
                        if stage == 0:
                            last = dve.max(v[:, 0:8], s)
                        elif stage == 1:
                            last = dve.match_replace(t, v[:, 0:8], s, LOW)
                        elif stage == 2:
                            last = dve.max(v[:, 8:16], t)
                        else:
                            dve.max_index(ix[:, 0:8], v[:, 0:8], s)
                            last = dve.max_index(ix[:, 8:16], v[:, 8:16], t)
                    then(last)

            for h in range(PH):
                for p in range(2):
                    dve.wait_ge(sc_done, 2 * h + p + 1)
                    sixteen_best(TC, lambda c: topv[:, p, c], lambda c: topi[:, p, c],
                                 lambda c: ps[:, 6 + p, c * P:(c + 1) * P], lambda c: tmp8[:, c])
                    dve.tensor_copy(tf[:, p, :, h], topi[:, p]).then_inc(sc_used, 1)
                dve.tensor_tensor(
                    cand[:], topv[:, 0].unsqueeze(3).broadcast_to([P, TC, TOPK, TOPK]),
                    topv[:, 1].unsqueeze(2).broadcast_to([P, TC, TOPK, TOPK]), ALU.add).then_inc(cand_done, 1)
                dve.wait_ge(cand_done, h + 1)
                sixteen_best(TC, lambda c: best[:, c, h], lambda c: pos[:, c],
                             lambda c: cand[:, c].rearrange("p a b -> p (a b)"), lambda c: tmpc[:, c])
                dve.tensor_scalar(kk[:, 0], pos[:], 4, None, ALU.logical_shift_right)
                then(dve.tensor_scalar(kk[:, 1], pos[:], TOPK - 1, None, ALU.bitwise_and))
                for w in range(2):
                    last = dve.tensor_copy(kf[:, w, :, h], kk[:, w])
            then(last)
            then(dve.tensor_copy(gsum[:], best[:, :, :, 0]))
            b3 = best[:].rearrange("p c h k -> p (c h) k")
            g3 = gsum[:].rearrange("p c h -> p (c h)").unsqueeze(2).broadcast_to([P, TC * PH, TOPK])
            dve.tensor_tensor(b3, b3, g3, ALU.subtract).then_inc(shifted, 1)

            def onehot16(w, tc):
                return dve.tensor_tensor(
                    oh16[:, w].rearrange("p h k m -> p (h k) m"),
                    kf[:, w, tc].rearrange("p h k -> p (h k)").unsqueeze(2).broadcast_to([P, PH * TOPK, TOPK]),
                    iota[:, 0:TOPK].unsqueeze(1).broadcast_to([P, PH * TOPK, TOPK]), ALU.is_equal)

            def pick(w, tc):
                return dve.tensor_reduce(ij[:, w, tc].rearrange("p h k -> p (h k)"),
                                         oh16[:, w].rearrange("p h k m -> p (h k) m"), AX.X, ALU.add)

            for tc in range(TC):
                onehot16(0, tc).then_inc(ohk_done, 1)
                then(onehot16(1, tc))
                then(dve.tensor_tensor(oh16[:, 1], oh16[:, 1], tf[:, 1, tc].unsqueeze(2).broadcast_to(
                    [P, PH, TOPK, TOPK]), ALU.mult))
                pick(1, tc).then_inc(ij_done, 1)
                dve.wait_ge(ohk_mul, tc + 1)
                pick(0, tc).then_inc(ij_done, 1)
                dve.wait_ge(ij_done, 2 * tc + 2)
            dve.wait_ge(g_exp, 1)
            then(dve.tensor_reduce(gsum[:].rearrange("p c h -> p (c h)"), b3, AX.X, ALU.add))
            then(dve.reciprocal(gsum[:], gsum[:]))
            dve.tensor_tensor(b3, b3, g3, ALU.mult).then_inc(gates_done, 1)
            dve.wait_ge(tr_out, 3)

            def columns(g, slot, again):
                if again:
                    dve.wait_ge(oh_used, g - 3)
                dve.tensor_tensor(oh_i[:, slot], iota[:].unsqueeze(1).broadcast_to([P, GRP, P]),
                                  iT[:, bass.ds(g * GRP, GRP)].unsqueeze(2).broadcast_to([P, GRP, P]), ALU.is_equal)
                for u in range(GRP):
                    t = bass.ds(g * GRP + u, 1)
                    last = dve.tensor_scalar(oh_g[:, slot, u], iota[:], jT[:, t], gT[:, t], ALU.is_equal, ALU.mult)
                last.then_inc(oh_done, 1)
            for g in range(4):
                columns(g, g, False)
            with dve.Fori(1, T // GRP // 4) as i:
                for slot in range(4):
                    columns(i * 4 + slot, slot, True)

            def gate_block(q, par, fill, ready):
                dve.wait_ge(*ready)
                dve.wait_ge(gate_in_sem[par], fill * 16)
                c = geluT[:, par].rearrange("p j (c t) -> p j c t", t=STG)
                dve.tensor_tensor(c, c, gate_in[:, par].rearrange("p c j t -> p j c t"),
                                  ALU.mult).then_inc(c_mul, 1)

            def made(q):
                return acc_free, q * BT + (S_U + (STORED + 1) * BT)

            def fetched(par, fill):
                return gelu_in[par], (fill - TURNS_U // 2) * 16

            def low_of_c(q, par):
                dve.wait_ge(c_hi_done, q + 1)
                dve.tensor_tensor(c_lo[:, par], geluT[:, par], c_hi[:, par].bitcast(F32),
                                  ALU.subtract).then_inc(c_lo_done, 1)

            def low_of_v(q, half, second=False):
                dve.wait_ge(v_hi_done, q * 2 + half + 1)
                lo, hi = (v_lo2, v_hi2) if second else (v_lo, v_hi)
                dve.tensor_tensor(lo[:], v_raw[:, half], hi[:].bitcast(F32), ALU.subtract).then_inc(v_lo_done, 1)

            def add_out(q, half):
                for m in range(OUT_BANKS):
                    dve.wait_ge(y_done, q * 8 + (half * OUT_BANKS + m + 1))
                    dve.tensor_tensor(x1T[:, half * OUT_BANKS + m], ps[:, Y_BANK + m],
                                      x1T[:, half * OUT_BANKS + m], ALU.add).then_inc(y_out, 1)

            dve.wait_ge(stage_out[0], 16 * (NSTG // 2))
            dve.wait_ge(gate_out, OUT_BANKS + T // GRP)
            dve.engine_nop().then_inc(y_out, OUT_BANKS)
            low_of_v(0, 0)
            gate_block(0, 0, 1, made(0))
            dve.wait_ge(stage_out[1], 16 * (NSTG // 2))
            low_of_c(0, 0)

            def step(q, par, fill, ready):
                gate_block(q + 1, 1 - par, fill, ready)
                low_of_c(q + 1, 1 - par)
                add_out(q, 0)
                low_of_v(q, 1)
                add_out(q, 1)
                low_of_v(q + 1, 0)

            def stored_step(q, par, fill, ready=None):
                low_of_v(q, 1, True)
                if fill is not None:
                    gate_block(q + 1, 1 - par, fill, ready or fetched(1 - par, fill))
                add_out(q, 0)
                if fill is not None:
                    low_of_c(q + 1, 1 - par)
                    low_of_v(q + 1, 0)
                add_out(q, 1)

            with dve.Fori(0, LOOP_U // 2) as i:
                for par in range(2):
                    q = i * 2 + par
                    step(q, par, i + (1 + par), made(q + 1))
            for q in range(LOOP_U, TURNS_U - AHEAD):
                step(q, q % 2, (q + 1) // 2 + 1, made(q + 1))
            stored_step(TURNS_U - 2, 0, TURNS_U // 2, made(TURNS_U - 1))
            stored_step(TURNS_U - 1, 1, TURNS_U // 2 + 1)
            with dve.Fori(TURNS_U // 2, NBLK // 2 - 1) as i:
                for par in range(2):
                    stored_step(i * 2 + par, par, i + (1 + par))
            stored_step(NBLK - 2, 0, NBLK // 2)
            stored_step(NBLK - 1, 1, None)
            norm(2)


def kernel(x, norm_mix, w_in, w_pool, pool_scale, w_out, norm_ffn, w_query, sub_keys, expert_u, expert_v, norm_final):
    import numpy as np
    import concourse.bacc as bacc
    from concourse.bass_utils import run_bass_kernel_spmd

    f = np.ascontiguousarray
    tiles = lambda w, m: f(np.asarray(w).reshape(KD, P, m, P).transpose(2, 1, 0, 3))
    w_in = np.asarray(w_in)[0]
    qkp = np.concatenate([w_in[:, 0:1024], w_in[:, 1536:2048]], axis=1)
    col = lambda v, k: np.asarray(v).reshape(k, P).T
    vecs = f(np.concatenate([col(norm_mix, KD), col(norm_ffn, KD), col(norm_final, KD), col(pool_scale, 4)], axis=1))

    dist = np.arange(P)[:, None] + (T - P) - np.arange(T)[None, :]
    hold = np.zeros((P, T), np.float32)
    for window, dilation in ((128, 1), (512, 4), (2048, 16)):
        hold += ((dist >= 0) & (dist <= window) & (dist % dilation == 0)).astype(np.float32)
    rc = np.stack([1.0 / np.minimum(np.arange(1, PAD + 1), w) for w in WINDOWS]).astype(np.float32).reshape(1, -1)
    consts = f(np.concatenate([
        np.eye(P, dtype=np.float32), np.tile(np.arange(P, dtype=np.float32), (P, 1)), hold,
        np.where(hold > 0, 0.0, NEG).astype(np.float32), np.tile(rc, (P, 1))], axis=1))

    arrays = {
        "xT": f(np.asarray(x)[0].T.reshape(KD, P, T).transpose(1, 0, 2)),
        "w_qkp": tiles(qkp, N_IN),
        "w_v": f(w_in[:, 1024:1536].reshape(KD, P, T).transpose(1, 0, 2)),
        "w_pool": f(np.asarray(w_pool)[0].transpose(1, 0, 2)),
        "w_outq": tiles(np.asarray(w_out)[0], N_OUT),
        "w_uq": tiles(np.asarray(w_query)[0], N_Q),
        "sub_keysT": f(np.asarray(sub_keys)[0].reshape(2 * PH, P, P).transpose(2, 0, 1)),
        "expert_uT": f(np.asarray(expert_u)[0].reshape(P, P, KD, P).transpose(1, 3, 2, 0)),
        "expert_v": f(np.asarray(expert_v)[0]),
        "vecs": vecs,
        "consts": consts,
    }
    nc = bacc.Bacc("TRN2", target_bir_lowering=False, num_devices=1)
    aps = [nc.dram_tensor(n, a.shape, F32, kind="ExternalInput").ap() for n, a in arrays.items()]
    out = nc.dram_tensor("outT", (P, KD, T), F32, kind="ExternalOutput").ap()
    peer_block(nc, *aps, out)
    r = run_bass_kernel_spmd(nc, [arrays], core_ids=[0])
    y = np.asarray(r.results[0]["outT"])
    return f(y.transpose(1, 0, 2).reshape(D, T).T).reshape(1, T, D)
```

```python
from contextlib import ExitStack

import concourse.bass as bass
from concourse import mybir

ALU = mybir.AluOpType
ACT = mybir.ActivationFunctionType
AX = mybir.AxisListType
F32 = mybir.dt.float32
F32R = mybir.dt.float32r
U32 = mybir.dt.uint32

P = 128
D = 1024
T = 512
KD = D // P
TC = T // P
HEADS = 8
HD = 64
PH = 8
TOPK = 16
NEG = -1e30
EPS = 1e-6
WINDOWS = (2, 4, 8, 16)
PAD = 16

N_IN, N_OUT, N_Q = 12, 8, 16
S_OUT = N_IN
S_Q = S_OUT + N_OUT
BT = 4
B_PICK = 8
U_AMONG_Q = 16
U_BEHIND_Q = B_PICK * BT - U_AMONG_Q
S_UQ = S_Q + N_Q + U_AMONG_Q
S_U = S_Q + N_Q
RING = 4
NBLK = P // BT
STG = 64
NSTG = T // STG
GRP = 4
SG = STG // GRP
STORED = B_PICK + NSTG
assert STORED * 2 == NBLK
TURNS = NBLK
TILES_END = TURNS - 3
OUT_BANKS = 4
Y_BANK, ACC_BANK = 0, OUT_BANKS


def peer_block(nc, xT, w_qkp, w_v, w_pool, w_outq, w_uq, sub_keysT, expert_uT, expert_v, vecs, consts, outT):
    gates_dram = nc.dram_tensor("gates_dram", [NSTG, P, P * STG], F32, kind="Internal").ap()
    gelu_dram = nc.dram_tensor("gelu_dram", [STORED, P, BT * T], F32, kind="Internal").ap()
    ctx = ExitStack()
    with ctx:
        def sem(name):
            return ctx.enter_context(nc.semaphore(name))

        base = (nc.sbuf_base + 63) // 64 * 64
        top = nc.sbuf_usable_end
        arena = ctx.enter_context(nc.sbuf_tensor("arena", [P, (top - base - 64) // 4], F32))

        def at(name, shape, dt, offset):
            n = 4
            for s in shape[1:]:
                n *= s
            n = (n + 31) // 32 * 32
            assert base + offset + n <= top - 64, (name, offset + n)
            return nc.alloc_sbuf_tensor_at(name, shape, dt, offset=base + offset), offset + n

        o = 0
        x1T, o = at("x1T", [P, KD, T], F32, o)
        act_hi, o = at("act_hi", [P, KD, T], F32R, o)
        act_lo, o = at("act_lo", [P, KD, T], F32R, o)
        w_raw, o = at("w_raw", [P, RING, KD, P], F32, o)
        w_hi, o = at("w_hi", [P, RING, KD, P], F32R, o)
        v_hi2, _ = at("v_hi2", [P, BT, T], F32R, o - 4 * RING * KD * P)
        v_lo2, _ = at("v_lo2", [P, BT, T], F32R, o)
        w_lo, o = at("w_lo", [P, RING, KD, P], F32R, o)
        ident, o = at("ident", [P, P], F32, o)
        iota, o = at("iota", [P, P], F32, o)
        vec_sb, o = at("vec_sb", [P, 3 * KD + 4], F32, o)
        ones, o = at("ones", [P, P], F32, o)
        eps_sb, o = at("eps_sb", [P, 8], F32, o)
        cnt, _ = at("cnt", [P, T], F32, o)
        negm, _ = at("negm", [P, T], F32, o + 4 * T)
        wpl, _ = at("wpl", [P, 4, P], F32, o + 8 * T)
        iT, o = at("iT", [P, T], F32, o)
        jT, o = at("jT", [P, T], F32, o)
        gT, o = at("gT", [P, T], F32, o)
        pT, _ = at("pT", [P, 2, TC, T], F32, o)
        geluT, o = at("geluT", [P, 2, BT, T], F32, o)
        R = o
        v_raw, o = at("v_raw", [P, 2, BT, T], F32, R)
        v_hi, o = at("v_hi", [P, BT, T], F32R, o)
        v_lo, o = at("v_lo", [P, BT, T], F32R, o)
        c_parts, o = at("c_parts", [P, 2, 2, BT, T], F32R, o)
        c_hi, c_lo = ([c_parts[:, 1 - par, part] for par in range(2)] for part in range(2))
        gate_in, o = at("gate_in", [P, 2, NSTG, BT, STG], F32, o)
        sq, o = at("sq", [P, KD, T], F32, R)
        stat, o = at("stat", [P, 5, TC], F32, o)
        std, var, rstd, newton, rstd2 = (stat[:, i] for i in range(5))
        spare, o = at("spare", [P, 1], F32, o)
        sq_sum, o = at("sq_sum", [P, T], F32, o)
        RN = o
        qk_hi, o = at("qk_hi", [P, 8, T], F32R, R)
        v_tok, o = at("v_tok", [P, TC, T], F32, RN)
        zp, o = at("zp", [P, 4, PAD + T], F32, o)
        lvl, o = at("lvl", [P, 2, PAD + T], F32, o)
        rcw, o = at("rcw", [P, 4, PAD], F32, o)
        mx, o = at("mx", [P, 3, TC], F32, o)
        nb, o = at("nb", [P, 3, TC], F32, o)
        den, o = at("den", [P, 3, TC], F32, o)
        rden, o = at("rden", [P, 3, TC], F32, o)
        RM = o
        wv_raw, o = at("wv_raw", [P, 4, T], F32, RM)
        wv_hi, o = at("wv_hi", [P, 4, T], F32R, o)
        wv_lo, o = at("wv_lo", [P, 4, T], F32R, o)
        ptmp, o = at("ptmp", [P, 4, T], F32, o)
        qk_lo, o = at("qk_lo", [P, 8, T], F32R, o)
        AW = 10 * P
        SLOTS = 3
        pr, o = at("pr", [P, SLOTS, AW], F32, RM)
        skT, o = at("skT", [P, 2 * PH, P], F32, RN)
        q2, o = at("q2", [P, 2, T], F32, o)
        topv, o = at("topv", [P, 2, TC, TOPK], F32, o)
        topi, o = at("topi", [P, 2, TC, TOPK], U32, o)
        tmp8, o = at("tmp8", [P, TC, P], F32, o)
        cand, o = at("cand", [P, TC, TOPK, TOPK], F32, o)
        tmpc, o = at("tmpc", [P, TC, TOPK * TOPK], F32, o)
        pos, o = at("pos", [P, TC, TOPK], U32, o)
        kk, o = at("kk", [P, 2, TC, TOPK], U32, o)
        best, o = at("best", [P, TC, PH, TOPK], F32, o)
        kf, o = at("kf", [P, 2, TC, PH, TOPK], F32, o)
        tf, o = at("tf", [P, 2, TC, PH, TOPK], F32, o)
        ij, o = at("ij", [P, 2, TC, PH, TOPK], F32, o)
        gsum, o = at("gsum", [P, TC, PH], F32, o)
        oh16, _ = at("oh16", [P, 2, PH, TOPK, TOPK], F32, R)
        stage, o = at("stage", [P, 2, P, STG], F32, R)
        oh_i, o = at("oh_i", [P, 4, GRP, P], F32, o)
        oh_g, o = at("oh_g", [P, 4, GRP, P], F32, o)

        ps = ctx.enter_context(nc.psum_tensor("ps", [P, 8, T], F32))

        x_in = [sem(f"x_in{q}") for q in range(4)]
        norm_in = sem("norm_in")
        const_in = sem("const_in")
        w_in_sem = [sem(f"w_in{r}") for r in range(RING)]
        wv_in = [sem(f"wv_in{r}") for r in range(4)]
        pool_w_in = sem("pool_w_in")
        keys_in = sem("keys_in")
        v_in = [sem("v_in0"), sem("v_in1")]
        gate_in_sem = [sem("gate_in0"), sem("gate_in1")]
        gelu_out = [sem("gelu_out0"), sem("gelu_out1")]
        gelu_in = [sem("gelu_in0"), sem("gelu_in1")]
        stage_out = [sem("stage_out0"), sem("stage_out1")]
        stage_up = [sem("stage_up0"), sem("stage_up1")]
        out_done = sem("out_done")
        w_hi_done = sem("w_hi_done")
        w_lo_done = sem("w_lo_done")
        w_used = sem("w_used")
        acc_free = sem("acc_free")
        consts_set = sem("consts_set")
        sq_done = sem("sq_done")
        ssq_done = sem("ssq_done")
        std_done = sem("std_done")
        sq_added = sem("sq_added")
        root_in = sem("root_in")
        rstd_done = sem("rstd_done")
        normed = sem("normed")
        act_hi_done = sem("act_hi_done")
        act_lo_done = sem("act_lo_done")
        wv_hi_done = sem("wv_hi_done")
        wv_lo_done = sem("wv_lo_done")
        wv_used = sem("wv_used")
        qk_hi_done = sem("qk_hi_done")
        vtok_done = sem("vtok_done")
        s_done = sem("s_done")
        s_masked = sem("s_masked")
        nb_done = sem("nb_done")
        p_exp = sem("p_exp")
        p_cnt = sem("p_cnt")
        rden_done = sem("rden_done")
        p_norm = sem("p_norm")
        p_norm_last = sem("p_norm_last")
        pt_done = sem("pt_done")
        pt_out = sem("pt_out")
        o_done = sem("o_done")
        o_hi = sem("o_hi")
        o_lo = sem("o_lo")
        sums_done = sem("sums_done")
        pooled_done = sem("pooled_done")
        pmix_done = sem("pmix_done")
        pscaled = sem("pscaled")
        pmix_hi = sem("pmix_hi")
        pmix_lo = sem("pmix_lo")
        sc_done = sem("sc_done")
        sc_used = sem("sc_used")
        cand_done = sem("cand_done")
        ohk_done = sem("ohk_done")
        ohk_mul = sem("ohk_mul")
        ij_done = sem("ij_done")
        shifted = sem("shifted")
        g_exp = sem("g_exp")
        gates_done = sem("gates_done")
        tr_done = sem("tr_done")
        tr_out = sem("tr_out")
        oh_done = sem("oh_done")
        oh_used = sem("oh_used")
        gate_out = sem("gate_out")
        v_hi_done = sem("v_hi_done")
        v_lo_done = sem("v_lo_done")
        c_mul = sem("c_mul")
        c_hi_done = sem("c_hi_done")
        c_lo_done = sem("c_lo_done")
        y_done = sem("y_done")
        y_out = sem("y_out")
        dve_self = sem("dve_self")
        final_done = sem("final_done")

        block = ctx.enter_context(nc.Block())

        S_AT = ((1, 2 * P), (1, 0), (0, 0), (2, 0))
        S_FREE = (2, 2, 3, 4)
        P_AT = (0, P, 3 * P, 6 * P)
        O_BANK = [(7, 5)[h % 2] for h in range(HEADS - 1)] + [2]
        V_BANK = (3, 6, 7, 5)
        POOL_BANK = 4
        SUM_BANK, RSTD_BANK = 6, 7

        def w_source(s):
            if s < S_OUT:
                return w_qkp[s]
            if s < S_Q:
                return w_outq[s - S_OUT]
            if s < S_UQ:
                pair, r = divmod(s - S_Q, 4)
                return w_uq[2 * pair + r] if r < 2 else expert_uT[2 * pair + r - 2]
            return expert_uT[s - S_U]

        def last_of(block):
            return S_Q + 8 * block + 7 if block < U_AMONG_Q // BT else S_U + BT * block + BT - 1

        @block.sync
        def _(sp):
            def load_w(s, src=None, first=False):
                if not first:
                    sp.wait_ge(w_lo_done, s - RING + 1)
                slot = s % RING if isinstance(s, int) else None
                sp.dma_start(w_raw[:, slot], w_source(s)).then_inc(w_in_sem[slot], 16)

            for q in range(4):
                sp.dma_start(x1T[:, 2 * q:2 * q + 2], xT[:, 2 * q:2 * q + 2]).then_inc(x_in[q], 16)
            sp.dma_start(vec_sb[:], vecs).then_inc(norm_in, 16)
            sp.dma_start(ident[:], consts[:, 0:P]).then_inc(norm_in, 16)
            for s in range(RING):
                load_w(s, first=True)
            sp.dma_start(iota[:], consts[:, P:2 * P]).then_inc(const_in, 16)
            sp.dma_start(cnt[:], consts[:, 2 * P:2 * P + T]).then_inc(const_in, 16)
            sp.dma_start(negm[:], consts[:, 2 * P + T:2 * P + 2 * T]).then_inc(const_in, 16)
            sp.dma_start(rcw[:], consts[:, 2 * P + 2 * T:2 * P + 2 * T + 4 * PAD].rearrange(
                "p (a b) -> p a b", a=4)).then_inc(const_in, 16)
            for k in range(4):
                sp.dma_start(wv_raw[:, k], w_v[:, k]).then_inc(wv_in[k], 16)
            sp.dma_start(wpl[:], w_pool).then_inc(pool_w_in, 16)
            for s in range(RING, S_OUT + RING):
                load_w(s)
                if s >= S_OUT:
                    k = s - S_OUT + 4
                    sp.wait_ge(wv_lo_done, k - 3)
                    sp.dma_start(wv_raw[:, k % 4], w_v[:, k]).then_inc(wv_in[k % 4], 16)
            for s in range(S_OUT + RING, S_Q + RING):
                load_w(s)
            sp.wait_ge(o_lo, HEADS)
            sp.wait_ge(pmix_lo, 4)
            sp.dma_start(skT[:], sub_keysT).then_inc(keys_in, 16)

            def store_gelu(block, par, last):
                sp.wait_ge(acc_free, last + 1)
                sp.dma_start(gelu_dram[bass.ds(block, 1)].rearrange("o p n -> (o p) n"),
                             geluT[:, par].rearrange("p j t -> p (j t)")).then_inc(gelu_out[par], 16)

            stores = {last_of(b) + RING + 1: b for b in range(B_PICK)}
            for s in range(S_Q + RING, S_U + (B_PICK + 2) * BT):
                load_w(s)
                if s in stores:
                    store_gelu(stores[s], stores[s] % 2, last_of(stores[s]))

            def load_u(n, t):
                sp.wait_ge(w_lo_done, S_U + n * BT + t - RING + 1)
                sp.dma_start(w_raw[:, t], expert_uT[bass.ds(n * BT + t, 1)].rearrange(
                    "o p k m -> (o p) k m")).then_inc(w_in_sem[t], 16)

            def gate_buffer(c, b, between=None):
                for t in range(BT):
                    load_u(c + (B_PICK + 2), t)
                store_gelu(c + B_PICK, b, c * BT + (S_U + B_PICK * BT + 3))
                sp.wait_ge(gate_out, c * SG + (SG + OUT_BANKS))
                for up, done in ((1, stage_up), (0, stage_out)):
                    dst = gates_dram[bass.ds(c, 1)].rearrange("o p n -> (o p) n")
                    half = P // 2 * STG
                    sp.dma_start(dst[:, up * half:(up + 1) * half],
                                 stage[:, b, up * P // 2:(up + 1) * P // 2].rearrange("p j t -> p (j t)")).then_inc(
                                     done[b], 16)
                    if up and between is not None:
                        between()

            def load_gates(n, par):
                src = gates_dram[:, :, bass.ds(n * (BT * STG), BT * STG)].rearrange(
                    "c i (j t) -> i c (j t)", t=STG)
                sp.dma_start(gate_in[:, par].rearrange("p c j t -> p c (j t)"), src).then_inc(gate_in_sem[par], 16)

            def load_gelu(n, par):
                sp.dma_start(geluT[:, par].rearrange("p j t -> p (j t)"),
                             gelu_dram[bass.ds(n, 1)].rearrange("o p n -> (o p) n")).then_inc(gelu_in[par], 16)

            def load_v(n, half):
                src = expert_v.rearrange("(i j) d -> i j d", j=P)[:, bass.ds(n * BT, BT), half * T:(half + 1) * T]
                sp.dma_start(v_raw[:, half], src).then_inc(v_in[half], 16)

            def first_loads():
                for t in (0, 1):
                    load_u(STORED + 2, t)
                for b in range(2):
                    sp.wait_ge(stage_up[b], 16 * (NSTG // 2))
                load_gates(STORED, 0)
                sp.wait_ge(stage_out[0], 16 * (NSTG // 2))
                load_v(STORED, 0)

            with sp.Fori(0, NSTG // 2 - 1) as i:
                for b in range(2):
                    gate_buffer(i * 2 + b, b)
            gate_buffer(NSTG - 2, 0)
            gate_buffer(NSTG - 1, 1, between=first_loads)
            for t in (2, 3):
                load_u(STORED + 2, t)
            load_v(STORED, 1)
            for b in range(2):
                sp.wait_ge(gelu_out[b], 16 * (STORED // 2))
            load_gelu(0, 1)
            sp.wait_ge(stage_out[1], 16 * (NSTG // 2))
            load_gates(0, 1)
            for t in (0, 1):
                load_u(STORED + 3, t)

            def step(q, i, par):
                late = isinstance(i, int)
                nxt = i + STORED + 1 if par else i
                if not late or q + 2 < TURNS:
                    sp.wait_ge(c_mul, q + 1)
                    load_gates(i + 1 if par else i + STORED + 1, par)
                    if par:
                        sp.wait_ge(c_lo_done, q + 1)
                        load_gelu(i + 1, 1)
                for half in range(2):
                    if not late or q + 1 < TURNS:
                        sp.wait_ge(v_lo_done, q * 2 + half + 1)
                        load_v(nxt, half)
                    n, t = (i + STORED + 4, half) if par else (i + STORED + 3, 2 + half)
                    if not late or n < NBLK:
                        load_u(n, t)

            with sp.Fori(0, STORED - 4) as i:
                for par in range(2):
                    step(i * 2 + par, i, par)
            for q in range(2 * (STORED - 4), TURNS):
                step(q, q // 2, q % 2)
            for k in range(KD):
                sp.wait_ge(final_done, k + 1)
                sp.dma_start(outT[:, k], sq[:, k]).then_inc(out_done, 16)
            sp.wait_ge(out_done, KD * 16)

        @block.gpsimd
        def _(pool):
            pool.memset(ones[:], 1.0).then_inc(consts_set, 1)
            pool.memset(eps_sb[:], EPS).then_inc(consts_set, 1)
            pool.memset(zp[:, :, 0:PAD], 0.0).then_inc(consts_set, 1)

            def cut_lo(s, slot, checked=True):
                if checked:
                    pool.wait_ge(w_used, s - RING + 1)
                pool.wait_ge(w_hi_done, s + 1)
                pool.tensor_tensor(w_lo[:, slot], w_raw[:, slot], w_hi[:, slot].bitcast(F32),
                                   ALU.subtract).then_inc(w_lo_done, 1)

            for s in range(S_OUT + RING):
                cut_lo(s, s % RING, s >= RING)
            pool.wait_ge(acc_free, N_IN)
            done = 0
            for g in range(4):
                src = zp[:, g]
                for l in range(g + 1):
                    w = 1 << l
                    lo = 2 * w - 1
                    if done:
                        pool.wait_ge(sums_done, done)
                    if l == 0 and g:
                        pool.wait_ge(pooled_done, 3 * g)
                    dst = lvl[:, l % 2]
                    pool.tensor_tensor(dst[:, lo:PAD + T], src[:, lo:PAD + T], src[:, lo - w:PAD + T - w],
                                       ALU.add).then_inc(sums_done, 1)
                    done += 1
                    src = dst
            for h in range(HEADS):
                pool.wait_ge(rden_done, h + 1)
                for i in range(TC - 1):
                    a = pr[:, h % SLOTS, P_AT[i]:P_AT[i] + (i + 1) * P]
                    pool.tensor_scalar(a, a, rden[:, h % SLOTS, i:i + 1], None, ALU.mult).then_inc(p_norm, 1)
            for s in range(S_OUT + RING, S_UQ + RING):
                cut_lo(s, s % RING)
            for tc in range(TC):
                pool.wait_ge(ohk_done, tc + 1)
                pool.tensor_tensor(oh16[:, 0], oh16[:, 0], tf[:, 0, tc].unsqueeze(2).broadcast_to(
                    [P, PH, TOPK, TOPK]), ALU.mult).then_inc(ohk_mul, 1)
                for t in range(U_BEHIND_Q // TC):
                    s = S_UQ + RING + U_BEHIND_Q // TC * tc + t
                    cut_lo(s, s % RING)
            with pool.Fori(B_PICK + 1, NBLK) as n:
                for t in range(BT):
                    cut_lo(n * BT + (S_U + t), t)

        @block.scalar
        def _(act):
            def cut_hi(s, slot, uses):
                act.wait_ge(w_in_sem[slot], uses * 16)
                if not (isinstance(s, int) and s < RING):
                    act.wait_ge(w_used, s - RING + 1)
                act.activation(w_hi[:, slot], w_raw[:, slot], ACT.Copy).then_inc(w_hi_done, 1)

            def square(k):
                act.activation(sq[:, k], x1T[:, k], ACT.Square).then_inc(sq_done, 1)

            def root(n):
                act.wait_ge(ssq_done, n + 1)
                act.activation(std, ps[:, SUM_BANK, 0:TC], ACT.Sqrt, scale=1.0 / D, bias=eps_sb[:, 0:1]).then_inc(std_done, 1)

            def high_of_normed(n):
                for k in range(KD):
                    act.wait_ge(normed, n * KD + k + 1)
                    act.activation(act_hi[:, k], sq[:, k], ACT.Copy).then_inc(act_hi_done, 1)

            def load_roots():
                act.activation(spare[:, 0:1], eps_sb[:, 0:1], ACT.Sqrt)

            act.wait_ge(consts_set, 3)
            load_roots()
            for k in range(KD):
                act.wait_ge(x_in[k // 2], 16)
                square(k)
            for s in (0, 1):
                cut_hi(s, s, 1)
            root(0)
            for s in (2, 3):
                cut_hi(s, s, 1)
            high_of_normed(0)

            def wv_high(k):
                act.wait_ge(wv_in[k % 4], 16 * (k // 4 + 1))
                if k >= 4:
                    act.wait_ge(wv_used, k - 3)
                act.activation(wv_hi[:, k % 4], wv_raw[:, k % 4], ACT.Copy).then_inc(wv_hi_done, 1)

            for s in range(N_IN):
                act.wait_ge(w_used, s + 1)
                if s == 0:
                    act.wait_ge(act_lo_done, KD)
                if s == 8:
                    act.wait_ge(acc_free, 8)
                if s < 8:
                    act.activation(qk_hi[:, s], ps[:, ACC_BANK + s % 2], ACT.Copy).then_inc(qk_hi_done, 1)
                else:
                    act.activation(zp[:, s - 8, PAD:PAD + T], ps[:, ACC_BANK + s % 2], ACT.Copy).then_inc(acc_free, 1)
                cut_hi(s + RING, (s + RING) % RING, (s + RING) // RING + 1)
                if s >= N_IN - 4:
                    wv_high(s - N_IN + 4)
            for k in range(4, KD):
                wv_high(k)
            act.activation(spare[:, 0:1], eps_sb[:, 0:1], ACT.Exp)
            act.wait_ge(wv_used, KD)
            for tc in range(TC):
                act.activation(v_tok[:, tc], ps[:, V_BANK[tc]], ACT.Copy).then_inc(vtok_done, 1)

            def exps(h):
                act.wait_ge(nb_done, h + 1)
                for i in range(TC):
                    a = pr[:, h % SLOTS, P_AT[i]:P_AT[i] + (i + 1) * P]
                    act.activation(a, a, ACT.Exp, scale=HD ** -0.5, bias=nb[:, h % SLOTS, i:i + 1]).then_inc(p_exp, 1)

            def norm_last(h):
                act.wait_ge(rden_done, h + 1)
                a = pr[:, h % SLOTS, P_AT[TC - 1]:AW]
                act.activation(a, a, ACT.Copy, scale=rden[:, h % SLOTS, TC - 1:TC]).then_inc(p_norm_last, 1)

            def transposed_out(h):
                for i in range(TC):
                    act.wait_ge(pt_done, h * TC + i + 1)
                    if i == 0 and h >= 2:
                        act.wait_ge(o_done, h - 1)
                    act.activation(pT[:, h % 2, 0:i + 1, i * P:(i + 1) * P],
                                   ps[:, (3, 6)[i % 2], 0:(i + 1) * P].rearrange("p (a b) -> p a b", b=P),
                                   ACT.Copy).then_inc(pt_out, 1)

            def head_out(h):
                act.wait_ge(o_done, h + 1)
                b = HD * (h % 2)
                act.activation(act_hi[b:b + HD, h // 2], ps[b:b + HD, O_BANK[h]], ACT.Copy).then_inc(o_hi, 1)

            for h in range(HEADS + 3):
                if h == HEADS:
                    load_roots()
                if 2 <= h < HEADS + 2:
                    transposed_out(h - 2)
                if h < HEADS:
                    exps(h)
                if 1 <= h <= HEADS:
                    norm_last(h - 1)
                if h >= 3:
                    head_out(h - 3)
                if 2 <= h < 6:
                    g = h - 2
                    act.wait_ge(pscaled, g + 1)
                    act.activation(act_hi[:, 4 + g], ptmp[:, g], ACT.Copy).then_inc(pmix_hi, 1)
            for s in range(S_OUT, S_Q):
                if s >= S_OUT + 2:
                    act.wait_ge(acc_free, s - 1)
                    square(s - 2 - S_OUT)
                cut_hi(s + RING, (s + RING) % RING, (s + RING) // RING + 1)
            for k in (KD - 2, KD - 1):
                act.wait_ge(acc_free, S_OUT + k + 1)
                square(k)
            root(1)
            act.wait_ge(w_used, S_Q)
            high_of_normed(1)

            def gelu(u, slot, s, free=None):
                act.wait_ge(w_used, s + 1)
                if free is not None:
                    act.wait_ge(gelu_out[slot], free)
                act.activation(geluT[:, slot, u], ps[:, ACC_BANK + u % 2], ACT.Gelu).then_inc(acc_free, 1)

            for s in range(S_Q, S_UQ + (B_PICK * BT - U_AMONG_Q)):
                pair, part = divmod(s - S_Q, 4)
                if s < S_UQ and part < 2:
                    hp = 2 * pair + part
                    act.wait_ge(w_used, s + 1)
                    if hp >= 2:
                        act.wait_ge(sc_done, hp - 1)
                    act.activation(q2[:, hp % 2], ps[:, ACC_BANK + s % 2], ACT.Copy).then_inc(acc_free, 1)
                else:
                    u = 2 * pair + part - 2 if s < S_UQ else s - S_U
                    blk = u // BT
                    gelu(u % BT, blk % 2, s, 16 * (blk // 2) if u % BT == 0 and blk >= 2 else None)
                cut_hi(s + RING, (s + RING) % RING, (s + RING) // RING + 1)
                if s == S_UQ + 3:
                    act.wait_ge(shifted, 1)
                    act.activation(best[:], best[:], ACT.Exp).then_inc(g_exp, 1)
                if s == S_U + B_PICK * BT - 2:
                    act.wait_ge(tr_done, 1)
                    for w, out in enumerate((iT, jT, gT)):
                        act.activation(out[:], ps[:, w], ACT.Copy).then_inc(tr_out, 1)
            act.wait_ge(tr_out, 3)
            act.nop().then_inc(gate_out, OUT_BANKS)

            def gate_sums_out(half, b):
                c = half * 2 + b
                if not (isinstance(half, int) and half == 0):
                    act.wait_ge(stage_up[b], half * 16)
                    act.wait_ge(stage_out[b], half * 16)
                for g in range(SG):
                    act.wait_ge(oh_used, c * SG + (g + 1))
                    act.activation(stage[:, b, :, g * GRP:(g + 1) * GRP].rearrange("p j t -> p t j"),
                                   ps[:, g % 4].rearrange("p (t j) -> p t j", j=P), ACT.Copy).then_inc(gate_out, 1)
                    if g % 4 == 3:
                        t = g // 4
                        s = c * BT + (S_U + B_PICK * BT + t)
                        gelu(t, b, s, (half + B_PICK // 2) * 16 if t == 0 else None)
                        cut_hi(s + BT, t, c + (S_U // RING + B_PICK + 2))

            for b in range(2):
                gate_sums_out(0, b)
            with act.Fori(1, NSTG // 2) as i:
                for b in range(2):
                    gate_sums_out(i, b)

            def cut_v(n, half):
                act.wait_ge(v_in[half], (n + 1) * 16)
                act.activation(v_hi[:], v_raw[:, half], ACT.Copy).then_inc(v_hi_done, 1)

            def cut_c(n, par):
                act.wait_ge(c_mul, n + 1)
                act.activation(c_hi[par], geluT[:, par], ACT.Copy).then_inc(c_hi_done, 1)

            def cut_v2(q):
                act.wait_ge(v_in[1], (q + 1) * 16)
                act.activation(v_hi2[:], v_raw[:, 1], ACT.Copy).then_inc(v_hi_done, 1)

            def fresh_tile(n, t, cut=True):
                s = n * BT + (S_U + STORED * BT + t)
                gelu(t, 0, s)
                if cut:
                    cut_hi(s + BT, t, n + (S_U // RING + STORED + 2))

            act.wait_ge(gelu_out[0], 16 * (STORED // 2))
            for t in range(BT):
                fresh_tile(0, t)
            act.wait_ge(stage_up[1], 16 * (NSTG // 2))
            cut_c(0, 0)
            act.wait_ge(stage_up[0], 16 * (NSTG // 2))
            act.wait_ge(stage_out[0], 16 * (NSTG // 2))
            cut_v(0, 0)
            act.wait_ge(c_lo_done, 1)
            for t in (0, 1):
                fresh_tile(1, t)
            act.wait_ge(stage_out[1], 16 * (NSTG // 2))

            def step(q, i, par, cut=True):
                for half in range(2):
                    act.wait_ge(y_done, q * 8 + 4 * half + 4)
                    if half == 0:
                        cut_v(q, 1)
                        cut_c(q + 1, 1 - par)
                    else:
                        cut_v(q + 1, 0)
                    if par and half == 0:
                        act.wait_ge(c_lo_done, q + 2)
                    if par:
                        fresh_tile(i + 2, half, cut)
                    else:
                        fresh_tile(i + 1, 2 + half, cut)

            with act.Fori(0, STORED - 3) as i:
                for par in range(2):
                    step(i * 2 + par, i, par)
            for q in range(2 * (STORED - 3), TILES_END):
                step(q, q // 2, q % 2, cut=q < TILES_END - 2)
            for q in range(TILES_END, TURNS):
                cut_v2(q)
                if q + 1 < TURNS:
                    cut_c(q + 1, 1 - q % 2)
                act.wait_ge(y_done, q * 8 + 4)
                if q + 1 < TURNS:
                    cut_v(q + 1, 0)
                    act.wait_ge(y_done, q * 8 + 8)
            load_roots()
            for k in range(KD):
                act.wait_ge(y_out, OUT_BANKS + (NBLK - 1) * 8 + k + 1)
                square(k)
            root(2)

        @block.tensor
        def _(pe):
            def three(out, w, sl, m, start, stop):
                (wh, wl), (mh, ml) = w, m
                pe.matmul(out, wh[sl], mh, start=start, stop=False)
                pe.matmul(out, wh[sl], ml, start=False, stop=False)
                return pe.matmul(out, wl[sl], mh, start=False, stop=stop)

            def tile(s, slot, part=range(KD), order=(0, KD - 1)):
                if part[0] == order[0]:
                    pe.wait_ge(w_lo_done, s + 1)
                    pe.wait_ge(acc_free, s - 1)
                for k in part:
                    last = three(ps[:, ACC_BANK + slot % 2], (w_hi, w_lo), (slice(None), slot, k),
                                 (act_hi[:, k], act_lo[:, k]), k == order[0], k == order[1])
                if part[-1] == order[1]:
                    last.then_inc(w_used, 1)

            def sum_squares(n):
                pe.wait_ge(sq_added, (n + 1) * (KD - 1))
                for tc in range(TC):
                    last = pe.matmul(ps[:, SUM_BANK, tc:tc + 1], sq_sum[:, tc * P:(tc + 1) * P], ones[:, 0:1],
                                     start=True, stop=True)
                last.then_inc(ssq_done, 1)
                pe.wait_ge(root_in, n + 1)
                for tc in range(TC):
                    last = pe.transpose(ps[:, RSTD_BANK, tc * P:(tc + 1) * P],
                                        rstd2[:, tc:tc + 1].broadcast_to([P, P]), ident[:])
                last.then_inc(rstd_done, 1)

            def two_tiles(s, n, first=False):
                pe.wait_ge(w_lo_done, s + 2)
                if not first:
                    pe.wait_ge(acc_free, s)
                for k in range(KD):
                    pe.wait_ge(act_lo_done, n * KD + k + 1)
                    for d in range(2):
                        last = three(ps[:, ACC_BANK + (s + d) % 2], (w_hi, w_lo), (slice(None), (s + d) % RING, k),
                                     (act_hi[:, k], act_lo[:, k]), k == 0, k == KD - 1)
                        if k == KD - 1:
                            last.then_inc(w_used, 1)

            pe.wait_ge(consts_set, 3)
            pe.wait_ge(norm_in, 32)
            sum_squares(0)
            two_tiles(0, 0, True)
            for s in range(2, N_IN):
                tile(s, s % RING)
            for k in range(KD):
                pe.wait_ge(wv_lo_done, k + 1)
                for tc in range(TC):
                    if k == 0 and tc == TC - 1:
                        pe.wait_ge(acc_free, N_IN)
                    sl = slice(tc * P, (tc + 1) * P)
                    out = ps[:, V_BANK[tc]]
                    pe.matmul(out, act_hi[:, k, sl], wv_hi[:, k % 4], start=k == 0, stop=False)
                    pe.matmul(out, act_lo[:, k, sl], wv_hi[:, k % 4], start=False, stop=False)
                    last = pe.matmul(out, act_hi[:, k, sl], wv_lo[:, k % 4], start=False, stop=k == KD - 1)
                last.then_inc(wv_used, 1)

            def scores(h):
                b, c = HD * (h % 2), h // 2
                for i in range(TC):
                    if h:
                        pe.wait_ge(s_masked, (h - 1) * TC + S_FREE[i])
                    bank, col = S_AT[i]
                    w = (i + 1) * P
                    three(ps[:, bank, col:col + w], (qk_hi, qk_lo), (slice(b, b + HD), c, slice(i * P, (i + 1) * P)),
                          (qk_hi[b:b + HD, 4 + c, 0:w], qk_lo[b:b + HD, 4 + c, 0:w]), True, True).then_inc(s_done, 1)

            def transposes(h):
                if h == 0:
                    pe.wait_ge(vtok_done, TC)
                for i in range(TC):
                    n = h * TC + i
                    if i < TC - 1:
                        pe.wait_ge(p_norm, h * (TC - 1) + i + 1)
                    else:
                        pe.wait_ge(p_norm_last, h + 1)
                    if n >= 2:
                        pe.wait_ge(pt_out, n - 1)
                    for kb in range(i + 1):
                        a = P_AT[i] + kb * P
                        last = pe.transpose(ps[:, (3, 6)[i % 2], kb * P:(kb + 1) * P], pr[:, h % SLOTS, a:a + P],
                                            ident[:])
                    last.then_inc(pt_done, 1)

            def weighted(h):
                pe.wait_ge(pt_out, (h + 1) * TC)
                if h == HEADS - 1:
                    pe.wait_ge(s_masked, HEADS * TC)
                elif h >= 2:
                    pe.wait_ge(o_lo, h - 1)
                b = HD * (h % 2)
                for kb in range(TC):
                    last = pe.matmul(ps[b:b + HD, O_BANK[h], kb * P:T], v_tok[:, kb, h * HD:(h + 1) * HD],
                                     pT[:, h % 2, kb, kb * P:T], start=kb == 0, stop=kb == TC - 1)
                last.then_inc(o_done, 1)

            def pooling_mix(g):
                if g == 0:
                    pe.wait_ge(pool_w_in, 16)
                pe.wait_ge(pooled_done, 3 * g + 3)
                if g:
                    pe.wait_ge(pscaled, g)
                pe.matmul(ps[:, POOL_BANK], wpl[:, g], ptmp[:, g], start=True, stop=True).then_inc(pmix_done, 1)

            for h in range(HEADS + 3):
                if h < HEADS:
                    scores(h)
                if 1 <= h < 5:
                    pooling_mix(h - 1)
                if h == HEADS:
                    pe.wait_ge(pmix_lo, 4)
                    tile(S_OUT, S_OUT % RING, part=range(4, KD), order=(4, 3))
                if h == HEADS + 2:
                    pe.wait_ge(o_lo, HEADS - 2)
                    tile(S_OUT + 1, (S_OUT + 1) % RING, part=range(4, KD), order=(4, 3))
                if 2 <= h < HEADS + 2:
                    transposes(h - 2)
                if h >= 3:
                    weighted(h - 3)
            pe.wait_ge(o_lo, HEADS)
            for s in (S_OUT, S_OUT + 1):
                tile(s, s % RING, part=range(4), order=(4, 3))
            for s in range(S_OUT + 2, S_Q):
                tile(s, s % RING)
            sum_squares(1)

            def key_scores(hp):
                if hp == 0:
                    pe.wait_ge(keys_in, 16)
                s = S_Q + 4 * (hp // 2) + hp % 2
                pe.wait_ge(acc_free, s + 1)
                if hp >= 2:
                    pe.wait_ge(sc_used, hp - 1)
                for tc in range(TC):
                    last = pe.matmul(ps[:, 6 + hp % 2, tc * P:(tc + 1) * P], q2[:, hp % 2, tc * P:(tc + 1) * P],
                                     skT[:, hp], start=True, stop=True)
                last.then_inc(sc_done, 1)
                return last

            two_tiles(S_Q, 1)
            for s in range(S_Q, S_UQ):
                if s >= S_Q + 2:
                    tile(s, s % RING)
                pair, part = divmod(s - S_Q, 4)
                if part in (1, 2):
                    key_scores(2 * pair + part - 1)
            for s in range(S_UQ, S_U + B_PICK * BT - 1):
                tile(s, s % RING)
            pe.wait_ge(ij_done, 2 * TC)
            pe.wait_ge(gates_done, 1)
            for w in range(3):
                for tc in range(TC):
                    src = (ij[:, w, tc] if w < 2 else best[:, tc]).rearrange("p h k -> p (h k)")
                    last = pe.transpose(ps[:, w, tc * P:(tc + 1) * P], src, ident[:])
            last.then_inc(tr_done, 1)
            tile(S_U + B_PICK * BT - 1, RING - 1)

            def gate_group(g, slot):
                pe.wait_ge(oh_done, g + 1)
                pe.wait_ge(gate_out, g + 1)
                for u in range(GRP):
                    last = pe.matmul(ps[:, slot, u * P:(u + 1) * P], oh_i[:, slot, u], oh_g[:, slot, u],
                                     start=True, stop=True)
                last.then_inc(oh_used, 1)

            with pe.Fori(0, NSTG) as c:
                for pair in range(SG // 2):
                    for b in range(2):
                        gate_group(c * SG + (2 * pair + b), (2 * pair + b) % 4)
                    t, half = divmod(pair, 2)
                    tile(c * BT + (S_U + B_PICK * BT + t), t, part=range(half * KD // 2, (half + 1) * KD // 2))
            for s in range(S_U + STORED * BT, S_U + (STORED + 1) * BT + 2):
                tile(s, s % RING)

            def combine(q, half, par, v, by_bank=False):
                pe.wait_ge(v_lo_done, q * 2 + half + 1)
                if half == 0:
                    pe.wait_ge(c_lo_done, q + 1)
                steps = [(t, m) for t in range(BT) for m in range(OUT_BANKS)]
                for t, m in sorted(steps, key=lambda tm: tm[1]) if by_bank else steps:
                    if t == 0:
                        pe.wait_ge(y_out, q * 8 + (half * OUT_BANKS + m + 1))
                    last = three(ps[:, Y_BANK + m], v, (slice(None), t, slice(m * P, (m + 1) * P)),
                                 (c_hi[par][:, t], c_lo[par][:, t]), t == 0, t == BT - 1)
                    if t == BT - 1:
                        last.then_inc(y_done, 1)

            def step(q, i, par):
                for half in range(2):
                    combine(q, half, par, (v_hi, v_lo))
                    n, t = (i + 2, half) if par else (i + 1, 2 + half)
                    tile(n * BT + (S_U + STORED * BT + t), t)

            with pe.Fori(0, TILES_END // 2) as i:
                for par in range(2):
                    step(i * 2 + par, i, par)
            step(TILES_END - 1, TILES_END // 2, 0)
            for q in range(TILES_END, TURNS):
                combine(q, 0, q % 2, (v_hi, v_lo))
                combine(q, 1, q % 2, (v_hi2, v_lo2), by_bank=q == TURNS - 1)
            sum_squares(2)

        @block.vector
        def _(dve):
            count = [0]

            def then(ins):
                count[0] += 1
                ins.then_inc(dve_self, 1)
                dve.wait_ge(dve_self, count[0])

            def add_squares(n, k):
                dve.wait_ge(sq_done, n * KD + k + 1)
                if k > 1:
                    dve.wait_ge(sq_added, n * (KD - 1) + k - 1)
                dve.tensor_tensor(sq_sum[:], sq_sum[:] if k > 1 else sq[:, 0], sq[:, k], ALU.add).then_inc(sq_added, 1)

            def norm(n):
                dve.wait_ge(std_done, n + 1)
                dve.tensor_scalar(var, ps[:, SUM_BANK, 0:TC], 1.0 / D, EPS, ALU.mult, ALU.add)
                then(dve.reciprocal(rstd, std))
                then(dve.tensor_tensor(newton, rstd, rstd, ALU.mult))
                then(dve.tensor_tensor(newton, newton, var, ALU.mult))
                then(dve.tensor_scalar(newton, newton, -0.5, 1.5, ALU.mult, ALU.add))
                dve.tensor_tensor(rstd2, rstd, newton, ALU.mult).then_inc(root_in, 1)
                dve.wait_ge(rstd_done, n + 1)
                for k in range(KD + 2):
                    if k < KD:
                        dve.scalar_tensor_tensor(
                            sq[:, k], x1T[:, k], vec_sb[:, n * KD + k:n * KD + k + 1], ps[:, RSTD_BANK],
                            ALU.mult, ALU.mult).then_inc(normed if n < 2 else final_done, 1)
                    if k >= 2 and n < 2:
                        dve.wait_ge(act_hi_done, n * KD + k - 1)
                        dve.tensor_tensor(act_lo[:, k - 2], sq[:, k - 2], act_hi[:, k - 2].bitcast(F32),
                                          ALU.subtract).then_inc(act_lo_done, 1)

            for k in range(1, KD):
                add_squares(0, k)
            dve.wait_ge(norm_in, 32)
            norm(0)
            for s in range(8):
                dve.wait_ge(qk_hi_done, s + 1)
                dve.tensor_tensor(qk_lo[:, s], ps[:, ACC_BANK + s % 2], qk_hi[:, s].bitcast(F32),
                                  ALU.subtract).then_inc(acc_free, 1)
            dve.wait_ge(const_in, 4 * 16)

            def pooled(g):
                dve.wait_ge(sums_done, (g + 1) * (g + 2) // 2)
                s, z = lvl[:, g % 2, PAD:], zp[:, g, PAD:]
                dve.scalar_tensor_tensor(ptmp[:, g, PAD:], s[:, PAD:], 1.0 / WINDOWS[g], z[:, PAD:], ALU.mult,
                                         ALU.subtract).then_inc(pooled_done, 1)
                dve.tensor_tensor(ptmp[:, g, 0:PAD], s[:, 0:PAD], rcw[:, g], ALU.mult).then_inc(pooled_done, 1)
                dve.wait_ge(pooled_done, 3 * g + 2)
                dve.tensor_tensor(ptmp[:, g, 0:PAD], ptmp[:, g, 0:PAD], z[:, 0:PAD],
                                  ALU.subtract).then_inc(pooled_done, 1)

            for k in range(KD):
                dve.wait_ge(wv_hi_done, k + 1)
                if k >= 4:
                    dve.wait_ge(wv_used, k - 3)
                dve.tensor_tensor(wv_lo[:, k % 4], wv_raw[:, k % 4], wv_hi[:, k % 4].bitcast(F32),
                                  ALU.subtract).then_inc(wv_lo_done, 1)
                if k >= 4:
                    pooled(k - 4)
            dve.wait_ge(wv_used, KD)

            def mask(h):
                dve.wait_ge(s_done, (h + 1) * TC)
                if h >= SLOTS:
                    dve.wait_ge(pt_done, (h - SLOTS + 1) * TC)
                for i in range(TC):
                    bank, col = S_AT[i]
                    w = (i + 1) * P
                    dve.tensor_tensor_reduce(pr[:, h % SLOTS, P_AT[i]:P_AT[i] + w], ps[:, bank, col:col + w],
                                             negm[:, T - w:T], 1.0, -3e38, ALU.add, ALU.max,
                                             mx[:, h % SLOTS, i:i + 1]).then_inc(s_masked, 1)
                dve.wait_ge(s_masked, (h + 1) * TC)
                dve.tensor_scalar(nb[:, h % SLOTS], mx[:, h % SLOTS], -(HD ** -0.5), None, ALU.mult).then_inc(nb_done, 1)

            def weigh(h):
                for i in range(TC):
                    dve.wait_ge(p_exp, h * TC + i + 1)
                    w = (i + 1) * P
                    a = pr[:, h % SLOTS, P_AT[i]:P_AT[i] + w]
                    dve.tensor_tensor_reduce(a, a, cnt[:, T - w:T], 1.0, 0.0, ALU.mult, ALU.add,
                                             den[:, h % SLOTS, i:i + 1]).then_inc(p_cnt, 1)
                dve.wait_ge(p_cnt, (h + 1) * TC)
                dve.reciprocal(rden[:, h % SLOTS], den[:, h % SLOTS]).then_inc(rden_done, 1)

            def low_of_head(h):
                dve.wait_ge(o_hi, h + 1)
                b = HD * (h % 2)
                dve.tensor_tensor(act_lo[b:b + HD, h // 2], ps[b:b + HD, O_BANK[h]], act_hi[b:b + HD, h // 2].bitcast(F32),
                                  ALU.subtract).then_inc(o_lo, 1)

            def scale_pooling(g):
                dve.wait_ge(pmix_done, g + 1)
                dve.tensor_scalar(ptmp[:, g], ps[:, POOL_BANK], vec_sb[:, 3 * KD + g:3 * KD + g + 1], None,
                                  ALU.mult).then_inc(pscaled, 1)

            def low_of_pooling(g):
                dve.wait_ge(pmix_hi, g + 1)
                dve.tensor_tensor(act_lo[:, 4 + g], ptmp[:, g], act_hi[:, 4 + g].bitcast(F32),
                                  ALU.subtract).then_inc(pmix_lo, 1)

            for h in range(HEADS + 4):
                if 2 <= h < 6:
                    scale_pooling(h - 2)
                if 3 <= h < 7:
                    low_of_pooling(h - 3)
                if h < HEADS:
                    mask(h)
                if 1 <= h <= HEADS:
                    weigh(h - 1)
                if h >= 4:
                    low_of_head(h - 4)
            for m in range(N_OUT):
                dve.wait_ge(w_used, S_OUT + m + 1)
                dve.tensor_tensor(x1T[:, m], ps[:, ACC_BANK + m % 2], x1T[:, m], ALU.add).then_inc(acc_free, 1)
                if m >= 2:
                    add_squares(1, m - 1)
            add_squares(1, KD - 1)
            norm(1)

            LOW = -3.4028235e38
            def sixteen_best(n, values, index, source, spare):
                for stage in range(4):
                    for c in range(n):
                        v, ix, s, t = values(c), index(c), source(c), spare(c)
                        if stage == 0:
                            last = dve.max(v[:, 0:8], s)
                        elif stage == 1:
                            last = dve.match_replace(t, v[:, 0:8], s, LOW)
                        elif stage == 2:
                            last = dve.max(v[:, 8:16], t)
                        else:
                            dve.max_index(ix[:, 0:8], v[:, 0:8], s)
                            last = dve.max_index(ix[:, 8:16], v[:, 8:16], t)
                    then(last)

            for h in range(PH):
                for p in range(2):
                    dve.wait_ge(sc_done, 2 * h + p + 1)
                    sixteen_best(TC, lambda c: topv[:, p, c], lambda c: topi[:, p, c],
                                 lambda c: ps[:, 6 + p, c * P:(c + 1) * P], lambda c: tmp8[:, c])
                    dve.tensor_copy(tf[:, p, :, h], topi[:, p]).then_inc(sc_used, 1)
                dve.tensor_tensor(
                    cand[:], topv[:, 0].unsqueeze(3).broadcast_to([P, TC, TOPK, TOPK]),
                    topv[:, 1].unsqueeze(2).broadcast_to([P, TC, TOPK, TOPK]), ALU.add).then_inc(cand_done, 1)
                dve.wait_ge(cand_done, h + 1)
                sixteen_best(TC, lambda c: best[:, c, h], lambda c: pos[:, c],
                             lambda c: cand[:, c].rearrange("p a b -> p (a b)"), lambda c: tmpc[:, c])
                dve.tensor_scalar(kk[:, 0], pos[:], 4, None, ALU.logical_shift_right)
                then(dve.tensor_scalar(kk[:, 1], pos[:], TOPK - 1, None, ALU.bitwise_and))
                for w in range(2):
                    last = dve.tensor_copy(kf[:, w, :, h], kk[:, w])
            then(last)
            then(dve.tensor_copy(gsum[:], best[:, :, :, 0]))
            b3 = best[:].rearrange("p c h k -> p (c h) k")
            g3 = gsum[:].rearrange("p c h -> p (c h)").unsqueeze(2).broadcast_to([P, TC * PH, TOPK])
            dve.tensor_tensor(b3, b3, g3, ALU.subtract).then_inc(shifted, 1)

            def onehot16(w, tc):
                return dve.tensor_tensor(
                    oh16[:, w].rearrange("p h k m -> p (h k) m"),
                    kf[:, w, tc].rearrange("p h k -> p (h k)").unsqueeze(2).broadcast_to([P, PH * TOPK, TOPK]),
                    iota[:, 0:TOPK].unsqueeze(1).broadcast_to([P, PH * TOPK, TOPK]), ALU.is_equal)

            def pick(w, tc):
                return dve.tensor_reduce(ij[:, w, tc].rearrange("p h k -> p (h k)"),
                                         oh16[:, w].rearrange("p h k m -> p (h k) m"), AX.X, ALU.add)

            for tc in range(TC):
                onehot16(0, tc).then_inc(ohk_done, 1)
                then(onehot16(1, tc))
                then(dve.tensor_tensor(oh16[:, 1], oh16[:, 1], tf[:, 1, tc].unsqueeze(2).broadcast_to(
                    [P, PH, TOPK, TOPK]), ALU.mult))
                pick(1, tc).then_inc(ij_done, 1)
                dve.wait_ge(ohk_mul, tc + 1)
                pick(0, tc).then_inc(ij_done, 1)
                dve.wait_ge(ij_done, 2 * tc + 2)
            dve.wait_ge(g_exp, 1)
            then(dve.tensor_reduce(gsum[:].rearrange("p c h -> p (c h)"), b3, AX.X, ALU.add))
            then(dve.reciprocal(gsum[:], gsum[:]))
            dve.tensor_tensor(b3, b3, g3, ALU.mult).then_inc(gates_done, 1)
            dve.wait_ge(tr_out, 3)

            def columns(g, slot, again):
                if again:
                    dve.wait_ge(oh_used, g - 3)
                dve.tensor_tensor(oh_i[:, slot], iota[:].unsqueeze(1).broadcast_to([P, GRP, P]),
                                  iT[:, bass.ds(g * GRP, GRP)].unsqueeze(2).broadcast_to([P, GRP, P]), ALU.is_equal)
                for u in range(GRP):
                    t = bass.ds(g * GRP + u, 1)
                    last = dve.tensor_scalar(oh_g[:, slot, u], iota[:], jT[:, t], gT[:, t], ALU.is_equal, ALU.mult)
                last.then_inc(oh_done, 1)
            for g in range(4):
                columns(g, g, False)
            with dve.Fori(1, T // GRP // 4) as i:
                for slot in range(4):
                    columns(i * 4 + slot, slot, True)

            def gate_block(q, par, fill, ready):
                dve.wait_ge(*ready)
                dve.wait_ge(gate_in_sem[par], fill * 16)
                c = geluT[:, par].rearrange("p j (c t) -> p j c t", t=STG)
                dve.tensor_tensor(c, c, gate_in[:, par].rearrange("p c j t -> p j c t"),
                                  ALU.mult).then_inc(c_mul, 1)

            def made(n):
                return acc_free, n * BT + (S_U + (STORED + 1) * BT)

            def fetched(n):
                return gelu_in[1], (n + 1) * 16

            def low_of_c(q, par):
                dve.wait_ge(c_hi_done, q + 1)
                dve.tensor_tensor(c_lo[par], geluT[:, par], c_hi[par].bitcast(F32),
                                  ALU.subtract).then_inc(c_lo_done, 1)

            def low_of_v(q, half, second=False):
                dve.wait_ge(v_hi_done, q * 2 + half + 1)
                lo, hi = (v_lo2, v_hi2) if second else (v_lo, v_hi)
                dve.tensor_tensor(lo[:], v_raw[:, half], hi[:].bitcast(F32), ALU.subtract).then_inc(v_lo_done, 1)

            def add_out(q, half, adds=False):
                for m in range(OUT_BANKS):
                    dve.wait_ge(y_done, q * 8 + (half * OUT_BANKS + m + 1))
                    dve.tensor_tensor(x1T[:, half * OUT_BANKS + m], ps[:, Y_BANK + m],
                                      x1T[:, half * OUT_BANKS + m], ALU.add).then_inc(y_out, 1)
                    if adds and half * OUT_BANKS + m >= 2:
                        add_squares(2, half * OUT_BANKS + m - 1)
                if adds and half:
                    add_squares(2, KD - 1)

            dve.wait_ge(gate_out, OUT_BANKS + T // GRP)
            dve.engine_nop().then_inc(y_out, OUT_BANKS)
            gate_block(0, 0, 1, made(0))
            low_of_c(0, 0)
            low_of_v(0, 0)

            def step(q, i, par):
                add_out(q, 0)
                low_of_v(q, 1)
                if par:
                    gate_block(q + 1, 0, i + 2, made(i + 1))
                else:
                    gate_block(q + 1, 1, i + 1, fetched(i))
                low_of_c(q + 1, 1 - par)
                add_out(q, 1)
                low_of_v(q + 1, 0)

            with dve.Fori(0, TILES_END // 2) as i:
                for par in range(2):
                    step(i * 2 + par, i, par)
            step(TILES_END - 1, TILES_END // 2, 0)
            for q in range(TILES_END, TURNS):
                last = q == TURNS - 1
                low_of_v(q, 1, second=True)
                if not last:
                    n = (q + 1) // 2
                    gate_block(q + 1, 1 - q % 2, n + 1, fetched(n) if q % 2 == 0 else made(n))
                add_out(q, 0, adds=last)
                if not last:
                    low_of_c(q + 1, 1 - q % 2)
                    low_of_v(q + 1, 0)
                add_out(q, 1, adds=last)
            norm(2)


def kernel(x, norm_mix, w_in, w_pool, pool_scale, w_out, norm_ffn, w_query, sub_keys, expert_u, expert_v, norm_final):
    import numpy as np
    import concourse.bacc as bacc
    from concourse.bass_utils import run_bass_kernel_spmd

    f = np.ascontiguousarray
    tiles = lambda w, m: f(np.asarray(w).reshape(KD, P, m, P).transpose(2, 1, 0, 3))
    w_in = np.asarray(w_in)[0]
    qkp = np.concatenate([w_in[:, 0:1024], w_in[:, 1536:2048]], axis=1)
    col = lambda v, k: np.asarray(v).reshape(k, P).T
    vecs = f(np.concatenate([col(norm_mix, KD), col(norm_ffn, KD), col(norm_final, KD), col(pool_scale, 4)], axis=1))

    dist = np.arange(P)[:, None] + (T - P) - np.arange(T)[None, :]
    hold = np.zeros((P, T), np.float32)
    for window, dilation in ((128, 1), (512, 4), (2048, 16)):
        hold += ((dist >= 0) & (dist <= window) & (dist % dilation == 0)).astype(np.float32)
    rc = np.stack([1.0 / np.minimum(np.arange(1, PAD + 1), w) for w in WINDOWS]).astype(np.float32).reshape(1, -1)
    consts = f(np.concatenate([
        np.eye(P, dtype=np.float32), np.tile(np.arange(P, dtype=np.float32), (P, 1)), hold,
        np.where(hold > 0, 0.0, NEG).astype(np.float32), np.tile(rc, (P, 1))], axis=1))

    arrays = {
        "xT": f(np.asarray(x)[0].T.reshape(KD, P, T).transpose(1, 0, 2)),
        "w_qkp": tiles(qkp, N_IN),
        "w_v": f(w_in[:, 1024:1536].reshape(KD, P, T).transpose(1, 0, 2)),
        "w_pool": f(np.asarray(w_pool)[0].transpose(1, 0, 2)),
        "w_outq": tiles(np.asarray(w_out)[0], N_OUT),
        "w_uq": tiles(np.asarray(w_query)[0], N_Q),
        "sub_keysT": f(np.asarray(sub_keys)[0].reshape(2 * PH, P, P).transpose(2, 0, 1)),
        "expert_uT": f(np.asarray(expert_u)[0].reshape(P, P, KD, P).transpose(1, 3, 2, 0)),
        "expert_v": f(np.asarray(expert_v)[0]),
        "vecs": vecs,
        "consts": consts,
    }
    nc = bacc.Bacc("TRN2", target_bir_lowering=False, num_devices=1)
    aps = [nc.dram_tensor(n, a.shape, F32, kind="ExternalInput").ap() for n, a in arrays.items()]
    out = nc.dram_tensor("outT", (P, KD, T), F32, kind="ExternalOutput").ap()
    peer_block(nc, *aps, out)
    r = run_bass_kernel_spmd(nc, [arrays], core_ids=[0])
    y = np.asarray(r.results[0]["outT"])
    return f(y.transpose(1, 0, 2).reshape(D, T).T).reshape(1, T, D)
```
